# Optimizing a Trainium2 kernel written in Bass

```python
import jax, jax.numpy as jnp
from jax import lax
import numpy as np
import math

D_MODEL = 1024
BATCH = 1
SEQ = 256
DEPTH = 1

N_HEADS = 8
QK_NOPE_DIM = 64
QK_ROPE_DIM = 32
V_HEAD_DIM = 64
Q_LORA_RANK = 256
KV_LORA_RANK = 256
ROPE_THETA = 10000.0
ATTN_WIDTH = N_HEADS * V_HEAD_DIM
Q_BLOCK = 128
FOURIER_GROUPS = 8
FOURIER_GROUP_DIM = 64
FOURIER_WIDTH = FOURIER_GROUPS * FOURIER_GROUP_DIM
N_BRANCHES = 2
N_EXPERT_GROUPS = 4
EXPERTS_PER_GROUP = 8
N_EXPERTS = N_EXPERT_GROUPS * EXPERTS_PER_GROUP
TOP_K_INNER = 2
D_EXPERT = 256
N_ADA = 6
EPS = 1e-6

IN_SIZES = (Q_LORA_RANK, KV_LORA_RANK, QK_ROPE_DIM, FOURIER_WIDTH, N_BRANCHES * D_MODEL)
IN_SPLITS = tuple(int(v) for v in np.cumsum(IN_SIZES)[:-1])
IN_COLS = int(sum(IN_SIZES))


def rmsnorm(x, g):
    xf = x.astype(jnp.float32)
    r = lax.rsqrt(jnp.mean(xf * xf, axis=-1, keepdims=True) + EPS)
    return (xf * r * g.astype(jnp.float32)).astype(x.dtype)

def modulate(h, shift, scale):
    return h * (1.0 + scale[:, None, :]) + shift[:, None, :]

def rope_angles(positions):
    inv_freq = ROPE_THETA ** (-jnp.arange(0, QK_ROPE_DIM, 2, dtype=jnp.float32) / QK_ROPE_DIM)
    ang = positions.astype(jnp.float32)[..., None] * inv_freq
    return jnp.cos(ang), jnp.sin(ang)

def apply_rope(x, cos, sin):
    half = QK_ROPE_DIM // 2
    x1, x2 = x[..., :half], x[..., half:]
    cos = cos.astype(x.dtype)
    sin = sin.astype(x.dtype)
    return jnp.concatenate([x1 * cos - x2 * sin, x2 * cos + x1 * sin], axis=-1)

def mla_attention(q_lat, kv_lat, k_rope, positions, g_q, g_kv, w_uq, w_uk, w_uv):
    B, S, _ = q_lat.shape
    q_lat = rmsnorm(q_lat, g_q)
    kv_lat = rmsnorm(kv_lat, g_kv)
    q = jnp.einsum('bsr,rhd->bshd', q_lat, w_uq)
    q_nope, q_rope = q[..., :QK_NOPE_DIM], q[..., QK_NOPE_DIM:]
    k_nope = jnp.einsum('bsr,rhd->bshd', kv_lat, w_uk)
    v = jnp.einsum('bsr,rhd->bshd', kv_lat, w_uv)
    cos, sin = rope_angles(positions)
    q_rope = apply_rope(q_rope, cos[:, :, None, :], sin[:, :, None, :])
    k_rope = apply_rope(k_rope, cos, sin)
    scale = (QK_NOPE_DIM + QK_ROPE_DIM) ** -0.5
    nb = S // Q_BLOCK
    qn_blk = (q_nope * scale).reshape(B, nb, Q_BLOCK, N_HEADS, QK_NOPE_DIM).transpose(1, 0, 2, 3, 4)
    qr_blk = (q_rope * scale).reshape(B, nb, Q_BLOCK, N_HEADS, QK_ROPE_DIM).transpose(1, 0, 2, 3, 4)

    def attend(blk):
        qn, qr = blk
        s = (jnp.einsum('bqhd,bkhd->bhqk', qn, k_nope)
             + jnp.einsum('bqhd,bkd->bhqk', qr, k_rope))
        p = jax.nn.softmax(s.astype(jnp.float32), axis=-1).astype(v.dtype)
        return jnp.einsum('bhqk,bkhd->bqhd', p, v)

    o = lax.map(attend, (qn_blk, qr_blk))
    return o.transpose(1, 0, 2, 3, 4).reshape(B, S, ATTN_WIDTH)

def fourier_mix(u):
    B, S, _ = u.shape
    ug = u.astype(jnp.float32).reshape(B, S, FOURIER_GROUPS, FOURIER_GROUP_DIM)
    f = jnp.fft.fft2(ug, axes=(1, 3), norm='ortho').real
    return f.reshape(B, S, FOURIER_WIDTH).astype(u.dtype)

def hierarchical_moe(h, w_rg, b_rg, w_re, b_re, w_gate, w_up, w_down):
    B, S, D = h.shape
    t = h.reshape(B * S, D)
    g_logits = (t @ w_rg).astype(jnp.float32) + b_rg.astype(jnp.float32)
    g_prob = jax.nn.softmax(g_logits, axis=-1)
    g_sel = jnp.argmax(g_prob, axis=-1)
    g_p = jnp.take_along_axis(g_prob, g_sel[:, None], axis=-1)[:, 0]
    e_logits = jnp.einsum('td,dge->tge', t, w_re).astype(jnp.float32) + b_re.astype(jnp.float32)
    e_logits = jnp.take_along_axis(e_logits, g_sel[:, None, None], axis=1)[:, 0]
    e_prob = jax.nn.softmax(e_logits, axis=-1)
    top_p, top_i = lax.top_k(e_prob, TOP_K_INNER)
    top_p = top_p / jnp.sum(top_p, axis=-1, keepdims=True)
    weights = g_p[:, None] * top_p
    global_idx = g_sel[:, None] * EXPERTS_PER_GROUP + top_i
    combine = jnp.sum(jax.nn.one_hot(global_idx, N_EXPERTS, dtype=jnp.float32)
                      * weights[..., None], axis=1).astype(t.dtype)
    out = jnp.zeros_like(t)
    for e in range(N_EXPERTS):
        hid = jax.nn.silu(t @ w_gate[e]) * (t @ w_up[e])
        out = out + combine[:, e:e + 1] * (hid @ w_down[e])
    return out.reshape(B, S, D)

def first_inputs(seed: int = 0) -> dict:
    key = jax.random.key(seed)
    ks = jax.random.split(key, 32)
    f32 = jnp.float32
    L, D = DEPTH, D_MODEL

    def nrm(k, shape, fan_in, mult=1.0):
        return jax.random.normal(k, shape, f32) * (mult * fan_in ** -0.5)

    def gain(k, shape):
        return 1.0 + 0.02 * jax.random.normal(k, shape, f32)

    x = jax.random.normal(ks[0], (BATCH, SEQ, D), f32)
    c = jax.random.normal(ks[1], (BATCH, D), f32)
    positions = jnp.sort(jax.random.randint(ks[2], (BATCH, SEQ), 0, 4 * SEQ), axis=-1).astype(jnp.int32)
    return {
        "x": x,
        "c": c,
        "positions": positions,
        "w_ada": nrm(ks[3], (L, D, N_ADA * D), D, 0.5),
        "b_ada": 0.02 * jax.random.normal(ks[4], (L, N_ADA * D), f32),
        "g_norm_mix": gain(ks[5], (L, D)),
        "w_in": nrm(ks[6], (L, D, IN_COLS), D),
        "g_q_lat": gain(ks[7], (L, Q_LORA_RANK)),
        "g_kv_lat": gain(ks[8], (L, KV_LORA_RANK)),
        "w_uq": nrm(ks[9], (L, Q_LORA_RANK, N_HEADS, QK_NOPE_DIM + QK_ROPE_DIM), Q_LORA_RANK),
        "w_uk": nrm(ks[10], (L, KV_LORA_RANK, N_HEADS, QK_NOPE_DIM), KV_LORA_RANK),
        "w_uv": nrm(ks[11], (L, KV_LORA_RANK, N_HEADS, V_HEAD_DIM), KV_LORA_RANK),
        "w_branch_attn": nrm(ks[12], (L, ATTN_WIDTH, D), ATTN_WIDTH),
        "w_branch_fourier": nrm(ks[13], (L, FOURIER_WIDTH, D), FOURIER_WIDTH),
        "b_gates": 0.02 * jax.random.normal(ks[14], (L, N_BRANCHES * D), f32),
        "w_out": nrm(ks[15], (L, D, D), D),
        "g_norm_ffn": gain(ks[16], (L, D)),
        "w_router_group": nrm(ks[17], (L, D, N_EXPERT_GROUPS), D),
        "b_router_group": 0.01 * jax.random.normal(ks[18], (L, N_EXPERT_GROUPS), f32),
        "w_router_expert": nrm(ks[19], (L, D, N_EXPERT_GROUPS, EXPERTS_PER_GROUP), D),
        "b_router_expert": 0.01 * jax.random.normal(ks[20], (L, N_EXPERT_GROUPS, EXPERTS_PER_GROUP), f32),
        "w_expert_gate": nrm(ks[21], (L, N_EXPERTS, D, D_EXPERT), D),
        "w_expert_up": nrm(ks[22], (L, N_EXPERTS, D, D_EXPERT), D),
        "w_expert_down": nrm(ks[23], (L, N_EXPERTS, D_EXPERT, D), D_EXPERT),
        "w_ada_final": nrm(ks[24], (D, 2 * D), D, 0.5),
        "b_ada_final": 0.02 * jax.random.normal(ks[25], (2 * D,), f32),
        "g_norm_final": gain(ks[26], (D,)),
    }

def first_block(x, c, positions, w_ada, b_ada, g_norm_mix, w_in, g_q_lat, g_kv_lat,
              w_uq, w_uk, w_uv, w_branch_attn, w_branch_fourier, b_gates, w_out,
              g_norm_ffn, w_router_group, b_router_group, w_router_expert, b_router_expert,
              w_expert_gate, w_expert_up, w_expert_down, w_ada_final, b_ada_final, g_norm_final):
    h = x
    c_act = jax.nn.silu(c)
    for l in range(DEPTH):
        mod = c_act @ w_ada[l] + b_ada[l]
        sh1, sc1, gt1, sh2, sc2, gt2 = jnp.split(mod, N_ADA, axis=-1)

        u = modulate(rmsnorm(h, g_norm_mix[l]), sh1, sc1)
        z = u @ w_in[l]
        q_lat, kv_lat, k_rope, f_in, gate_logits = jnp.split(z, IN_SPLITS, axis=-1)
        a = mla_attention(q_lat, kv_lat, k_rope, positions, g_q_lat[l], g_kv_lat[l],
                          w_uq[l], w_uk[l], w_uv[l]) @ w_branch_attn[l]
        fo = fourier_mix(f_in) @ w_branch_fourier[l]
        ga, gf = jnp.split(gate_logits + b_gates[l], N_BRANCHES, axis=-1)
        merged = jax.nn.sigmoid(ga) * a + jax.nn.sigmoid(gf) * fo
        h = h + gt1[:, None, :] * (merged @ w_out[l])

        v = modulate(rmsnorm(h, g_norm_ffn[l]), sh2, sc2)
        h = h + gt2[:, None, :] * hierarchical_moe(
            v, w_router_group[l], b_router_group[l], w_router_expert[l], b_router_expert[l],
            w_expert_gate[l], w_expert_up[l], w_expert_down[l])

    fmod = c_act @ w_ada_final + b_ada_final
    shf, scf = jnp.split(fmod, 2, axis=-1)
    return modulate(rmsnorm(h, g_norm_final), shf, scf)


DEPTH_2 = 2

GRID_W = 64
CTX_LEN = 256
HEAD_DIM = 64
NA_HEADS = D_MODEL // 2 // HEAD_DIM
NA_WIN_ROWS = 8
NA_WIN_COLS = 16
DIFF_HEAD_DIM = 64
DIFF_V_DIM = 2 * DIFF_HEAD_DIM
DIFF_HEADS = D_MODEL // 2 // DIFF_V_DIM
NA_WIDTH = NA_HEADS * HEAD_DIM
DIFF_QK_WIDTH = DIFF_HEADS * 2 * DIFF_HEAD_DIM
DIFF_V_WIDTH = DIFF_HEADS * DIFF_V_DIM
ATTN_IN_WIDTH = 3 * NA_WIDTH + 2 * DIFF_QK_WIDTH + DIFF_V_WIDTH
ATTN_OUT_WIDTH = NA_WIDTH + DIFF_V_WIDTH
ATTN_SPLITS = [NA_WIDTH, 2 * NA_WIDTH, 3 * NA_WIDTH,
               3 * NA_WIDTH + DIFF_QK_WIDTH, 3 * NA_WIDTH + 2 * DIFF_QK_WIDTH]
CONV_WIDTH = 3
D_FF = 2816
ATTN_BLOCK = 128
N_MOD = 9
N_ATTN_LAYERS = (DEPTH_2 + 1) // 2
N_CONV_LAYERS = DEPTH_2 // 2
NEG_INF = -1e30


def rmsnorm_2(x, g):
    x32 = x.astype(jnp.float32)
    y = x32 * lax.rsqrt(jnp.mean(x32 * x32, axis=-1, keepdims=True) + EPS)
    return (y * g.astype(jnp.float32)).astype(x.dtype)

def modulate_2(x, g, shift, scale):
    return rmsnorm_2(x, g) * (1 + scale) + shift

def swiglu(x, w_gate, w_up, w_down):
    return (jax.nn.silu(x @ w_gate) * (x @ w_up)) @ w_down

def macaron_ffn(xs, g, shift, scale, gate, w_gate, w_up, w_down):
    return xs + 0.5 * gate * swiglu(modulate_2(xs, g, shift, scale), w_gate, w_up, w_down)

def axial_rope(n):
    t = jnp.arange(n)
    row = (t // GRID_W).astype(jnp.float32)
    col = (t % GRID_W).astype(jnp.float32)
    n_freq = DIFF_HEAD_DIM // 4
    inv = ROPE_THETA ** (-jnp.arange(n_freq, dtype=jnp.float32) / n_freq)
    ang = jnp.concatenate([row[:, None] * inv, col[:, None] * inv], axis=-1)
    return jnp.cos(ang)[:, None, None, :], jnp.sin(ang)[:, None, None, :]

def apply_rope_2(x, cos, sin):
    x32 = x.astype(jnp.float32)
    x1, x2 = x32[..., 0::2], x32[..., 1::2]
    out = jnp.stack([x1 * cos - x2 * sin, x1 * sin + x2 * cos], axis=-1)
    return out.reshape(x.shape).astype(x.dtype)

def split_attn_proj(p):
    b, t, _ = p.shape
    qa, ka, va, qb, kb, vb = jnp.split(p, ATTN_SPLITS, axis=-1)
    na = lambda a: a.reshape(b, t, NA_HEADS, HEAD_DIM)
    dqk = lambda a: a.reshape(b, t, DIFF_HEADS, 2, DIFF_HEAD_DIM)
    return (na(qa), na(ka), na(va), dqk(qb), dqk(kb), vb.reshape(b, t, DIFF_HEADS, DIFF_V_DIM))

def dense_attend(q, k, v):
    s = jnp.einsum('bqhd,bkhd->bhqk', q * q.shape[-1] ** -0.5, k)
    p = jax.nn.softmax(s.astype(jnp.float32), axis=-1).astype(v.dtype)
    return jnp.einsum('bhqk,bkhd->bqhd', p, v)

def diff_attend(q, k, v, lam):
    s = jnp.einsum('bqhmd,bkhmd->bhmqk', q * q.shape[-1] ** -0.5, k)
    p = jax.nn.softmax(s.astype(jnp.float32), axis=-1)
    pd = (p[:, :, 0] - lam * p[:, :, 1]).astype(v.dtype)
    return jnp.einsum('bhqk,bkhe->bqhe', pd, v)

def neighbourhood_attention(q, k, v, k_ctx, v_ctx, rpb):
    b, n, h, d = q.shape
    rows = n // GRID_W
    kr = min(NA_WIN_ROWS, rows)
    qg = (q * d ** -0.5).reshape(b, rows, GRID_W, h, d)
    kg = k.reshape(b, rows, GRID_W, h, d)
    vg = v.reshape(b, rows, GRID_W, h, d)
    qc = jnp.arange(GRID_W)
    col_start = jnp.clip(qc - NA_WIN_COLS // 2, 0, GRID_W - NA_WIN_COLS)
    col_mask = (qc[None, :] >= col_start[:, None]) & (qc[None, :] < col_start[:, None] + NA_WIN_COLS)
    dc_idx = jnp.clip(qc[None, :] - qc[:, None] + NA_WIN_COLS - 1, 0, 2 * NA_WIN_COLS - 2)

    def row_block(r):
        start = jnp.clip(r - kr // 2, 0, rows - kr)
        q_r = lax.dynamic_index_in_dim(qg, r, axis=1, keepdims=False)
        k_band = lax.dynamic_slice_in_dim(kg, start, kr, axis=1)
        v_band = lax.dynamic_slice_in_dim(vg, start, kr, axis=1)
        s_band = jnp.einsum('bqhd,brkhd->bhqrk', q_r, k_band).astype(jnp.float32)
        dr_idx = start + jnp.arange(kr) - r + NA_WIN_ROWS - 1
        bias = rpb[:, dr_idx[None, :, None], dc_idx[:, None, :]].astype(jnp.float32)
        s_band = jnp.where(col_mask[:, None, :], s_band + bias, NEG_INF)
        s_ctx = jnp.einsum('bqhd,blhd->bhql', q_r, k_ctx).astype(jnp.float32)
        s = jnp.concatenate([s_band.reshape(b, h, GRID_W, kr * GRID_W), s_ctx], axis=-1)
        p = jax.nn.softmax(s, axis=-1).astype(v.dtype)
        p_band = p[..., :kr * GRID_W].reshape(b, h, GRID_W, kr, GRID_W)
        p_ctx = p[..., kr * GRID_W:]
        return (jnp.einsum('bhqrk,brkhd->bqhd', p_band, v_band)
                + jnp.einsum('bhql,blhd->bqhd', p_ctx, v_ctx))

    out = lax.map(row_block, jnp.arange(rows))
    return jnp.moveaxis(out, 0, 1).reshape(b, n, h, d)

def attn_mixer(xn, xn_ctx, w_in, w_out, rpb, lam_vec, subln_g, lam_init, cos, sin, ctx_out):
    b, n, _ = xn.shape
    qa, ka, va, qb, kb, vb = split_attn_proj(xn @ w_in)
    qa_c, ka_c, va_c, qb_c, kb_c, vb_c = split_attn_proj(xn_ctx @ w_in)
    qb, kb = apply_rope_2(qb, cos, sin), apply_rope_2(kb, cos, sin)
    l32 = lam_vec.astype(jnp.float32)
    lam = jnp.exp(jnp.sum(l32[0] * l32[1])) - jnp.exp(jnp.sum(l32[2] * l32[3])) + lam_init

    a_lat = neighbourhood_attention(qa, ka, va, ka_c, va_c, rpb)
    k_all = jnp.concatenate([kb, kb_c], axis=1)
    v_all = jnp.concatenate([vb, vb_c], axis=1)
    nb = n // ATTN_BLOCK
    q_blocks = jnp.moveaxis(qb.reshape(b, nb, ATTN_BLOCK, DIFF_HEADS, 2, DIFF_HEAD_DIM), 1, 0)
    d_lat = lax.map(lambda q_blk: diff_attend(q_blk, k_all, v_all, lam), q_blocks)
    d_lat = jnp.moveaxis(d_lat, 0, 1).reshape(b, n, DIFF_HEADS, DIFF_V_DIM)

    def merge(a, dd):
        t = a.shape[1]
        dd = rmsnorm_2(dd, subln_g) * (1.0 - lam_init)
        return jnp.concatenate([a.reshape(b, t, NA_WIDTH), dd.reshape(b, t, DIFF_V_WIDTH)], axis=-1) @ w_out

    y_lat = merge(a_lat, d_lat)
    if ctx_out:
        y_ctx = merge(dense_attend(qa_c, ka_c, va_c), diff_attend(qb_c, kb_c, vb_c, lam))
    else:
        y_ctx = None
    return y_lat, y_ctx

def conv_mixer(xn, w_in, w_out, conv_w):
    bg, cg, h = jnp.split(xn @ w_in, 3, axis=-1)
    u = cg * h
    v = lax.conv_general_dilated(u, conv_w[:, None, :].astype(u.dtype), window_strides=(1,),
                                 padding=((CONV_WIDTH // 2, CONV_WIDTH // 2),),
                                 dimension_numbers=('NWC', 'WIO', 'NWC'),
                                 feature_group_count=u.shape[-1])
    return (bg * v) @ w_out

def second_inputs(seed: int = 0) -> dict:
    key = jax.random.key(seed)
    ks = jax.random.split(key, 20)
    nrm = lambda k, shape, s: jax.random.normal(k, shape, jnp.float32) * s
    D = D_MODEL
    return {
        "x": nrm(ks[0], (BATCH, SEQ, D), 1.0),
        "c": nrm(ks[1], (BATCH, D), 1.0),
        "ctx": nrm(ks[2], (BATCH, CTX_LEN, D), 1.0),
        "c_ctx": nrm(ks[3], (D,), 1.0),
        "mod_w": nrm(ks[4], (DEPTH_2, D, N_MOD * D), D ** -0.5),
        "mod_b": nrm(ks[5], (DEPTH_2, N_MOD * D), 0.01),
        "norm_g": 1.0 + nrm(ks[6], (DEPTH_2, 3, D), 0.1),
        "ffn_w_gate": nrm(ks[7], (DEPTH_2, 2, D, D_FF), D ** -0.5),
        "ffn_w_up": nrm(ks[8], (DEPTH_2, 2, D, D_FF), D ** -0.5),
        "ffn_w_down": nrm(ks[9], (DEPTH_2, 2, D_FF, D), D_FF ** -0.5),
        "attn_w_in": nrm(ks[10], (N_ATTN_LAYERS, D, ATTN_IN_WIDTH), D ** -0.5),
        "attn_w_out": nrm(ks[11], (N_ATTN_LAYERS, ATTN_OUT_WIDTH, D), ATTN_OUT_WIDTH ** -0.5),
        "na_rpb": nrm(ks[12], (N_ATTN_LAYERS, NA_HEADS, 2 * NA_WIN_ROWS - 1, 2 * NA_WIN_COLS - 1), 0.2),
        "diff_lambda": nrm(ks[13], (N_ATTN_LAYERS, 4, DIFF_HEAD_DIM), 0.1),
        "diff_subln_g": 1.0 + nrm(ks[14], (N_ATTN_LAYERS, DIFF_V_DIM), 0.1),
        "conv_w_in": nrm(ks[15], (N_CONV_LAYERS, D, 3 * D), D ** -0.5),
        "conv_w_out": nrm(ks[16], (N_CONV_LAYERS, D, D), D ** -0.5),
        "conv_w": nrm(ks[17], (N_CONV_LAYERS, CONV_WIDTH, D), CONV_WIDTH ** -0.5),
        "final_g": 1.0 + nrm(ks[18], (D,), 0.1),
    }

def second_block(x, c, ctx, c_ctx, mod_w, mod_b, norm_g, ffn_w_gate, ffn_w_up, ffn_w_down,
              attn_w_in, attn_w_out, na_rpb, diff_lambda, diff_subln_g,
              conv_w_in, conv_w_out, conv_w, final_g):
    n = x.shape[1]
    cos, sin = axial_rope(n)
    x_lat, x_ctx = x, ctx
    for i in range(DEPTH_2):
        last = i == DEPTH_2 - 1
        is_attn = i % 2 == 0
        ctx_live = is_attn or not last
        j = i // 2
        m = jnp.split((jax.nn.silu(c) @ mod_w[i] + mod_b[i])[:, None, :], N_MOD, axis=-1)
        if ctx_live:
            mc = jnp.split(jax.nn.silu(c_ctx) @ mod_w[i] + mod_b[i], N_MOD, axis=-1)

        x_lat = macaron_ffn(x_lat, norm_g[i, 0], m[0], m[1], m[2],
                            ffn_w_gate[i, 0], ffn_w_up[i, 0], ffn_w_down[i, 0])
        if ctx_live:
            x_ctx = macaron_ffn(x_ctx, norm_g[i, 0], mc[0], mc[1], mc[2],
                                ffn_w_gate[i, 0], ffn_w_up[i, 0], ffn_w_down[i, 0])

        xn = modulate_2(x_lat, norm_g[i, 1], m[3], m[4])
        if is_attn:
            xn_c = modulate_2(x_ctx, norm_g[i, 1], mc[3], mc[4])
            lam_init = 0.8 - 0.6 * math.exp(-0.3 * i)
            y, y_c = attn_mixer(xn, xn_c, attn_w_in[j], attn_w_out[j], na_rpb[j], diff_lambda[j],
                                diff_subln_g[j], lam_init, cos, sin, ctx_out=not last)
        else:
            y = conv_mixer(xn, conv_w_in[j], conv_w_out[j], conv_w[j])
            if not last:
                y_c = conv_mixer(modulate_2(x_ctx, norm_g[i, 1], mc[3], mc[4]),
                                 conv_w_in[j], conv_w_out[j], conv_w[j])
        x_lat = x_lat + m[5] * y
        if not last:
            x_ctx = x_ctx + mc[5] * y_c

        x_lat = macaron_ffn(x_lat, norm_g[i, 2], m[6], m[7], m[8],
                            ffn_w_gate[i, 1], ffn_w_up[i, 1], ffn_w_down[i, 1])
        if not last:
            x_ctx = macaron_ffn(x_ctx, norm_g[i, 2], mc[6], mc[7], mc[8],
                                ffn_w_gate[i, 1], ffn_w_up[i, 1], ffn_w_down[i, 1])
    return rmsnorm_2(x_lat, final_g)


def setup_inputs(seed=0):
    out = dict(first_inputs(seed))
    for name, value in second_inputs(seed + 1).items():
        if name != "x":
            out[name + "_2"] = value
    return out


def reference(
    x, c, positions, w_ada, b_ada, g_norm_mix, w_in, g_q_lat, g_kv_lat, w_uq, w_uk, w_uv,
    w_branch_attn, w_branch_fourier, b_gates, w_out, g_norm_ffn, w_router_group, b_router_group,
    w_router_expert, b_router_expert, w_expert_gate, w_expert_up, w_expert_down, w_ada_final,
    b_ada_final, g_norm_final, c_2, ctx_2, c_ctx_2, mod_w_2, mod_b_2, norm_g_2, ffn_w_gate_2,
    ffn_w_up_2, ffn_w_down_2, attn_w_in_2, attn_w_out_2, na_rpb_2, diff_lambda_2,
    diff_subln_g_2, conv_w_in_2, conv_w_out_2, conv_w_2, final_g_2,
):
    x = first_block(
        x, c, positions, w_ada, b_ada, g_norm_mix, w_in, g_q_lat, g_kv_lat, w_uq, w_uk, w_uv,
        w_branch_attn, w_branch_fourier, b_gates, w_out, g_norm_ffn, w_router_group,
        b_router_group, w_router_expert, b_router_expert, w_expert_gate, w_expert_up,
        w_expert_down, w_ada_final, b_ada_final, g_norm_final,
    )
    return second_block(
        x, c_2, ctx_2, c_ctx_2, mod_w_2, mod_b_2, norm_g_2, ffn_w_gate_2, ffn_w_up_2,
        ffn_w_down_2, attn_w_in_2, attn_w_out_2, na_rpb_2, diff_lambda_2, diff_subln_g_2,
        conv_w_in_2, conv_w_out_2, conv_w_2, final_g_2,
    )


_drawn_inputs = setup_inputs


def setup_inputs(seed=0):
    import zlib

    import numpy as np

    out = dict(_drawn_inputs(seed))
    spreads = {}
    factors = {'g_norm_mix': 8.0,
     'g_q_lat': 8.0,
     'g_kv_lat': 8.0,
     'b_gates': 8.0,
     'g_norm_ffn': 2.821,
     'b_router_group': 6.133,
     'b_router_expert': 8.0,
     'na_rpb_2': 6.134}
    for name, (base, spread) in spreads.items():
        noise = np.random.default_rng([zlib.crc32(name.encode()), seed]).standard_normal(out[name].shape)
        drawn = base * np.exp(spread * noise) if base else spread * noise
        out[name] = __import__('jax').numpy.asarray(drawn.astype(out[name].dtype))
    for name, factor in factors.items():
        out[name] = (out[name] * factor).astype(out[name].dtype)
    return out
```

```python
import concourse.bass as bass
from concourse import mybir
from contextlib import ExitStack
import numpy as np

P = 128
D = 1024
KD = D // P
S = 256
TB = S // P
EPS = 1e-6
H1, NOPE, ROPE, VD = 8, 64, 32, 64
QKD = NOPE + ROPE
LORA = 256
KL = LORA // P
NG, NE8 = 4, 8
NEXP = NG * NE8
FU = 256
D_FF = 2816
FF_UNITS = D_FF // FU
NA_H, DF_H, HD = 8, 4, 64
NKT = 2 * TB
GRID = 64
LAM_INIT = 0.2
NEG = -1e30
PAGE = 2048
PAGE_SLOTS = 8
UNIT_PAGES = 4

ADA, FIN, MOD0, MOD1 = 0, 48, 64, 136
NMOD = 208
_o = 0
VCOL = {}
for _n, _w in (("g_mix", 8), ("g_ffn", 8), ("g_fin1", 8), ("norm_g", 48), ("g_fin2", 8), ("b_gates", 16),
               ("conv_w", 24), ("g_q", 2), ("g_kv", 2), ("c", 24), ("subln", 1)):
    VCOL[_n] = _o
    _o += _w
NVEC = _o

PAGE_AT, _n = {}, 0
for _name, _c in (("ada_a", 8), ("win_q", 1), ("win_kv", 1), ("win_f", 2), ("win_g", 8), ("uq", 1), ("uk", 1),
                  ("uv", 1), ("ada_b", 16), ("br", 4), ("wout", 4), ("ada_f", 8), ("moe", NEXP * 4),
                  ("m0_tail", 4), ("ctx_ff", FF_UNITS * 4), ("ff00", FF_UNITS * 4), ("proj", 12),
                  ("m1_tail", 3), ("aout", 4), ("ff01", FF_UNITS * 4), ("ff10", FF_UNITS * 4), ("cin", 12),
                  ("cout", 4), ("ff11", FF_UNITS * 4)):
    PAGE_AT[_name] = _n
    _n += _c
NPAGES = _n


def build(nc, pages, acts, vecs, mbias, small):
    f32, bf16, i32 = mybir.dt.float32, mybir.dt.bfloat16, mybir.dt.int32
    ALU, ACT, AX = mybir.AluOpType, mybir.ActivationFunctionType, mybir.AxisListType

    ctx = ExitStack()
    with ctx:
        def sb(name, shape, dt=f32):
            return ctx.enter_context(nc.sbuf_tensor(name, shape, dt))

        sems = {}

        def sem(name):
            if name not in sems:
                sems[name] = ctx.enter_context(nc.semaphore(name))
            return sems[name]

        ring = sb("ring", [P, PAGE_SLOTS, PAGE])
        HT = sb("HT", [P, KD, S])
        CT = sb("CT", [P, KD, S])
        Y = sb("Y", [P, KD, S])
        YC = sb("YC", [P, KD, S])
        XR = sb("XR", [P, KD, S])
        RT = sb("RT", [P, 2 * S])
        RI = sb("RI", [P, 2 * S])
        NA_ = sb("NA_", [P, KD])
        HG = sb("HG", [P, KD])
        MODT = sb("MODT", [P, NMOD, 2])
        MB = sb("MB", [P, NMOD, 2])
        V = sb("V", [P, NVEC])
        CA = sb("CA", [P, KD, 3])
        EPSC = sb("EPSC", [P, 1])
        ONES = sb("ONES", [P, P])
        ZW = sb("ZW", [P, P], bf16)
        ZX = sb("ZX", [P, 512], bf16)
        SIL = sb("SIL", [P, 2, S])
        TG = sb("TG", [P, 2, S])
        HID = sb("HID", [P, 2, 2, S])
        CMASK = sb("CMASK", [NEXP, 2, S])
        COMBT = sb("COMBT", [NEXP, S])
        IDENT = sb("IDENT", [P, P])
        ROTB = sb("ROTB", [P, P])
        CSB = sb("CSB", [P, 2, S])
        WRT = sb("WRT", [P, KD, NG + NEXP])
        BRT = sb("BRT", [P, NG + NEXP])
        REV = sb("REV", [P, NE8])
        INVF = sb("INVF", [QKD, 1])
        CTf, YCf = CT[:].rearrange("p k t -> p (k t)"), YC[:].rearrange("p k t -> p (k t)")
        DFTS = CTf[:, 0:1024].rearrange("p (t c n) -> p t c n", t=TB, c=2)
        DFTD = CTf[:, 1024:1280].rearrange("p (c n) -> p c n", c=2)
        WKR = CTf[:, 1280:1536].rearrange("p (k n) -> p k n", k=KD)
        ROTA = CTf[0:QKD, 1536:1536 + QKD]
        POSI = YCf[0:QKD, 0:S].bitcast(i32)
        ANG = YCf[0:QKD, 256:768].rearrange("p (a t) -> p a t", a=2)
        AK = YCf[0:QKD, 768:1280].rearrange("p (a t) -> p a t", a=2)
        CSA = YCf[0:QKD, 1280:1792].rearrange("p (a t) -> p a t", a=2)
        BT = sb("BT", [P, NA_H, 6, GRID])
        MASK = sb("MASK", [P, GRID])
        LAMV = sb("LAMV", [P, 4, HD])
        LAMT = sb("LAMT", [P, 8])
        ST = sb("ST", [P, 32])
        R = sb("R", [P, 16640])

        def reg(off, *dims, parts=P):
            n = int(np.prod(dims))
            v = R[0:parts, off:off + n]
            names = "abcd"[:len(dims)]
            if len(dims) == 1:
                return v
            return v.rearrange(f"p ({' '.join(names)}) -> p {' '.join(names)}",
                               **{names[i]: dims[i] for i in range(1, len(dims))})

        G = reg(0, 16, S)
        QL = reg(4096, 4, S)
        QK = reg(5120, 9, S, parts=QKD)
        KH = reg(7424, H1, S, parts=QKD)
        RW = reg(4096, 8, 80)
        V1 = reg(9472, TB, H1 * VD)
        FT = reg(10496, 4, S)
        U2 = reg(11520, TB, 2, 512)
        FO = reg(10496, 4, S)
        P1 = reg(13568, 2, TB, S)
        PT1 = reg(14592, 2, TB, S)
        AT = reg(15616, 4, S)
        QA = reg(0, 4, S)
        KA = reg(1024, 4, 2 * S)
        VA = reg(3072, NKT, 512)
        QB = reg(5120, 4, S)
        KB = reg(6144, 4, 2 * S)
        VB = reg(8192, NKT, 512)
        P2 = reg(10240, 2, 2, 512)
        PT2 = reg(12288, 2, NKT, S)
        MG = reg(14336, KD, S)
        CG = reg(0, KD, S)
        UU = reg(2048, KD, S + 2)
        VV = reg(4112, KD, S)
        BV = reg(6160, KD, S)

        PS = [ctx.enter_context(nc.psum_tensor(f"bank{b}", [P, 512], f32)) for b in range(8)]
        ACC, GU, MODB, MISC = (0, 1, 2, 3), (4, 5), 6, 7

        slot = [sem(f"page_in_{i}") for i in range(PAGE_SLOTS)]
        s_page = sem("page_used")
        s_tile = sem("tile_done")
        s_fa = sem("act_read_tile")
        s_fd = sem("dve_read_tile")
        s_modev = sem("mod_taken")
        s_hid = sem("hid_done")
        s_silu = sem("silu_done")
        s_sq, s_ss = sem("norm_squares"), sem("norm_sum")
        s_rt, s_ri, s_xr, s_y = sem("norm_root"), sem("norm_coef"), sem("norm_scaled"), sem("norm_out")
        s_ac, s_dc = sem("act_chain"), sem("dve_chain")

        tiles, order = {}, []
        freed = {"act": 0, "dve": 0}
        done = [0]

        def tile(name, n, banks, reader, page=None, own=None, free=None):
            for i in range(n):
                if own is not None:
                    ready = own
                elif page is None:
                    done[0] += 1
                    ready = (s_tile, done[0])
                else:
                    ready = (s_page, (page(i) if callable(page) else page + i) + 1)
                if free is not None:
                    rel = free(i)
                else:
                    freed[reader] += 1
                    rel = ({"act": s_fa, "dve": s_fd}[reader], freed[reader])
                b = banks[i % len(banks)]
                tiles[name, i] = (b, ready, rel)
                order.append((name, i))

        PA = PAGE_AT
        LB = (0, 1, 2, 3)
        tile("ss0", 1, (MISC,), "act")
        tile("q", 1, (0,), "act", PA["win_q"])
        tile("kv", 1, (1,), "act", PA["win_kv"])
        tile("kr", 1, (2,), "act")
        tile("f", 2, (3, 4), "dve", PA["win_f"])
        tile("sslat", 1, (MISC,), "act")
        tile("g", 8, (0, 1, 2, 3), "act", PA["win_g"])
        for h in range(4):
            tile(f"qh{h}", 1, ((4, 5)[h % 2],), "act", page=PA["uq"] if h == 3 else None)
        for h in range(4):
            tile(f"kh{h}", 1, ((4, 5)[h % 2],), "dve", page=PA["uk"] if h == 3 else None)
        tile("v0", 1, (0,), "dve")
        tile("v1", 1, (1,), "dve", PA["uv"])
        tile("rot", 5, (2, 3, 4, 5, 7), "dve")
        for h in range(H1):
            tile(f"s{h}", 1, ((0, 1)[h % 2],), None, free=lambda i, h=h: (sem("exp1"), h + 1))
            if h >= 1:
                tile(f"pt{h - 1}", 1, (2,), None, free=lambda i, h=h: (sem("pt1"), h))
                if (h - 1) % 2 == 0:
                    tile(f"o{(h - 1) // 2}", 1, ((3, 7)[((h - 1) // 2) % 2],), "dve",
                         own=(sem("o1_done"), (h - 1) // 2 + 1))
        tile("pt7", 1, (2,), None, free=lambda i: (sem("pt1"), 8))
        tile("fd", 4, (4, 5), "dve")
        tile("fs", 2, (0, 1), "dve")
        tile("bra", 4, (2, 3), "dve", page=lambda i: PA["br"] + i // 2)
        tile("brf", 4, (4, 5), "dve", page=lambda i: PA["br"] + 2 + i // 2)
        tile("wout", 4, (0, 1), "dve", PA["wout"])
        tile("ss1", 1, (MISC,), "act")
        tile("rt", 1, (0,), "dve")
        tile("ct", 1, (1,), "dve")
        tile("acc_moe", 4, ACC, "dve", page=lambda i: PA["moe"] + NEXP * 4 - 1)
        tile("ss2", 1, (MISC,), "act")
        tile("ss3", 1, (4,), "act")
        tile("ss4", 1, (MISC,), "act")
        tile("acc_ctx", 4, ACC, "dve", page=lambda i: PA["ctx_ff"] + FF_UNITS * 4 - 1)
        tile("acc_00", 4, ACC, "dve", page=lambda i: PA["ff00"] + FF_UNITS * 4 - 1)
        tile("ss5", 1, (4,), "act")
        tile("ss6", 1, (MISC,), "act")
        tile("qa", 2, (0, 1), "act", PA["proj"])
        for i in range(2):
            tile(f"ka{i}", 2, ((2, 3), (4, 5))[i], "act", page=lambda j, i=i: PA["proj"] + 2 + i)
        for i in range(2):
            tile(f"va{i}", 2, ((0, 1), (2, 3))[i], "dve", page=lambda j, i=i: PA["proj"] + 4 + i)
        tile("qb", 2, (4, 5), "act", PA["proj"] + 6)
        for i in range(2):
            tile(f"kb{i}", 2, ((0, 1), (2, 3))[i], "act", page=lambda j, i=i: PA["proj"] + 8 + i)
        for i in range(2):
            tile(f"vb{i}", 2, ((4, 5), (0, 1))[i], "dve", page=lambda j, i=i: PA["proj"] + 10 + i)
        tile("rotb", 4, (2, 3, 4, 5), "dve")
        NA_N = NA_H * TB
        for a in range(NA_N + 1):
            if a < NA_N:
                tile(f"sa{a}", 1, ((0, 1)[a % 2],), None, free=lambda i, a=a: (sem("exp2"), a + 1))
            if a >= 1:
                tile(f"pta{a - 1}", 1, ((2, 3)[(a - 1) % 2],), None, free=lambda i, a=a: (sem("pt2"), a))
                if (a - 1) % 4 == 1:
                    tile(f"oa{(a - 1) // 4}", 1, ((4, 5)[((a - 1) // 4) % 2],), "dve",
                         own=(sem("oa_done"), (a - 1) // 4 + 1))
        DF_N = DF_H * TB
        for a in range(DF_N + 1):
            if a < DF_N:
                for m in range(2):
                    tile(f"sd{2 * a + m}", 1, ((0, 1, 4, 5)[(2 * a + m) % 4],), None,
                         free=lambda i, a=a, m=m: (sem("exp3"), 2 * a + m + 1))
            if a >= 1:
                tile(f"ptd{a - 1}", 1, ((2, 3)[(a - 1) % 2],), None, free=lambda i, a=a: (sem("pt3"), a))
                if (a - 1) % 2 == 1:
                    tile(f"od{(a - 1) // 2}", 1, (MISC,), "dve")
        tile("sssub", 2, (0, 1), "act")
        tile("aout", 4, (2, 3), "dve", PA["aout"])
        tile("ss7", 1, (MISC,), "act")
        tile("acc_01", 4, ACC, "dve", page=lambda i: PA["ff01"] + FF_UNITS * 4 - 1)
        tile("ss8", 1, (MISC,), "act")
        tile("acc_10", 4, ACC, "dve", page=lambda i: PA["ff10"] + FF_UNITS * 4 - 1)
        tile("ss9", 1, (MISC,), "act")
        for i in range(4):
            tile(f"cg{i}", 1, ((0, 1)[i % 2],), "act", page=lambda j, i=i: PA["cin"] + 2 * i)
            tile(f"ch{i}", 1, ((2, 3)[i % 2],), "dve", page=lambda j, i=i: PA["cin"] + 2 * i + 1)
        tile("cb", 4, (4, 5), "dve", PA["cin"] + 8)
        tile("cout", 4, (0, 1), "dve", PA["cout"])
        tile("ss10", 1, (MISC,), "act")
        tile("acc_11", 4, ACC, "dve", page=lambda i: PA["ff11"] + FF_UNITS * 4 - 1)
        tile("ss11", 1, (MISC,), "act")

        prev_free, last = {}, {}
        for key in order:
            b, _, rel = tiles[key]
            prev_free[key] = last.get(b)
            last[b] = rel

        def bank(name, i=0):
            return PS[tiles[name, i][0]]

        def opened(pe, name, i=0):
            if prev_free[name, i] is not None:
                pe.wait_ge(*prev_free[name, i])
            return bank(name, i)

        def filled(eng, name, i=0):
            eng.wait_ge(*tiles[name, i][1])
            return bank(name, i)

        NORMS = [
            (HT, Y, "g_mix", 0, ADA + 8, ADA, 0),
            (HT, Y, "g_ffn", 0, ADA + 32, ADA + 24, 0),
            (HT, HT, "g_fin1", 0, FIN + 8, FIN, 0),
            (CT, YC, "norm_g", 0, MOD0 + 8, MOD0, 1),
            (HT, Y, "norm_g", 0, MOD0 + 8, MOD0, 0),
            (CT, YC, "norm_g", 8, MOD0 + 32, MOD0 + 24, 1),
            (HT, Y, "norm_g", 8, MOD0 + 32, MOD0 + 24, 0),
            (HT, Y, "norm_g", 16, MOD0 + 56, MOD0 + 48, 0),
            (HT, Y, "norm_g", 24, MOD1 + 8, MOD1, 0),
            (HT, Y, "norm_g", 32, MOD1 + 32, MOD1 + 24, 0),
            (HT, Y, "norm_g", 40, MOD1 + 56, MOD1 + 48, 0),
            (HT, Y, "g_fin2", 0, None, None, 0),
        ]
        NCH = 4

        PASSES, _u = {}, 0
        for name, n, m, src, routed in (
                ("moe", NEXP, MOD0, Y, True), ("ctx_ff", FF_UNITS, MOD1, YC, False),
                ("ff00", FF_UNITS, MOD1 + 2 * FF_UNITS, Y, False), ("ff01", FF_UNITS, MOD1 + 4 * FF_UNITS, Y, False),
                ("ff10", FF_UNITS, None, Y, False), ("ff11", FF_UNITS, None, Y, False)):
            PASSES[name] = (PA[name], _u, n, m, src, routed)
            _u += n

        MOD_GROUPS = {"ada_a": (ADA, 8, 1), "ada_b": (ADA + 16, 2, 8), "ada_f": (FIN, 8, 1), "moe": (MOD0, 1, NEXP),
                      "m0_tail": (MOD0 + 64, 4, 1), "ctx_ff": (MOD1, 1, 11), "ff00": (MOD1 + 22, 1, 11),
                      "m1_tail": (MOD1 + 44, 3, 1), "ff01": (MOD1 + 50, 1, 11)}
        MOD_BEFORE, _g = {}, 0
        for name, (_, _, n) in MOD_GROUPS.items():
            MOD_BEFORE[name] = _g
            _g += n
        PASSES["ff01"] = PASSES["ff01"][:3] + (MOD1 + 50,) + PASSES["ff01"][4:]

        block = ctx.enter_context(nc.Block())

        @block.sync
        def _(sp):
            def page(p, wait=None):
                if wait is not None:
                    sp.wait_ge(s_page, wait)
                return p

            holes = set()
            for name in ("ff10", "ff11"):
                for u in range(FF_UNITS):
                    holes.add(PA[name] + 4 * u + 2)

            def run(p0, p1):
                p = p0
                while p < p1 and (p < PAGE_SLOTS or p % PAGE_SLOTS or p1 - p < 2 * PAGE_SLOTS):
                    one(p)
                    p += 1
                turns = (p1 - p) // PAGE_SLOTS
                if turns > 1:
                    with sp.Fori(0, turns) as i:
                        for j in range(PAGE_SLOTS):
                            if p + j in holes:
                                continue
                            sp.wait_ge(s_page, i * PAGE_SLOTS + (p + j + 1 - PAGE_SLOTS))
                            sp.dma_start(ring[:, j, :], pages[i * PAGE_SLOTS + (p + j)]).then_inc(slot[j], 16)
                    p += turns * PAGE_SLOTS
                while p < p1:
                    one(p)
                    p += 1

            def one(p):
                if p in holes:
                    return
                if p >= PAGE_SLOTS:
                    sp.wait_ge(s_page, p + 1 - PAGE_SLOTS)
                sp.dma_start(ring[:, p % PAGE_SLOTS, :], pages[p]).then_inc(slot[p % PAGE_SLOTS], 16)

            run(0, PA["ff10"])
            run(PA["ff10"], PA["cin"])
            run(PA["cin"], PA["ff11"])
            run(PA["ff11"], NPAGES)

        holes_before = {}
        for j in range(PAGE_SLOTS):
            holes_before[j] = sorted(PA[n] + 4 * u + 2 for n in ("ff10", "ff11") for u in range(FF_UNITS)
                                     if (PA[n] + 4 * u + 2) % PAGE_SLOTS == j)

        def arrived(pe, p, i=0, stride=0):
            j = p % PAGE_SLOTS
            n = p // PAGE_SLOTS + 1 - sum(1 for x in holes_before[j] if x < p)
            pe.wait_ge(slot[j], i * stride + 16 * n)
            return ring[:, j, :]

        @block.gpsimd
        def _(pool):
            nc.gpsimd.dma_start(V[:], vecs).then_inc(sem("in_vecs"), 16)
            nc.gpsimd.dma_start(HT[:], acts[0]).then_inc(sem("in_x"), 16)
            nc.gpsimd.dma_start(MB[:], mbias).then_inc(sem("in_mb"), 16)
            nc.gpsimd.dma_start(WKR[:], small["wkr"]).then_inc(sem("in_small"), 16)
            nc.gpsimd.dma_start(ROTA[:], small["rota"]).then_inc(sem("in_small"), 16)
            nc.gpsimd.dma_start(INVF[:], small["invf"]).then_inc(sem("in_small"), 16)
            nc.gpsimd.dma_start(POSI[:], small["pos"].partition_broadcast(QKD)).then_inc(sem("in_small"), 16)
            nc.gpsimd.dma_start(DFTD[:], small["dftd"]).then_inc(sem("in_small"), 16)
            nc.gpsimd.dma_start(DFTS[:], small["dfts"]).then_inc(sem("in_small"), 16)
            nc.gpsimd.dma_start(IDENT[:], small["ident"]).then_inc(sem("in_small"), 16)
            nc.gpsimd.dma_start(WRT[:], small["wrt"]).then_inc(sem("in_small"), 16)
            nc.gpsimd.dma_start(BRT[:], small["brt"].partition_broadcast(P)).then_inc(sem("in_small"), 16)
            nc.gpsimd.dma_start(REV[:], small["rev"].partition_broadcast(P)).then_inc(sem("in_small"), 16)
            pool.wait_ge(sem("comb"), 1)
            nc.gpsimd.dma_start(CT[:], acts[1]).then_inc(sem("in_late"), 16)
            nc.gpsimd.dma_start(ROTB[:], small["rotb"]).then_inc(sem("in_late"), 16)
            nc.gpsimd.dma_start(CSB[:], small["csb"]).then_inc(sem("in_late"), 16)
            nc.gpsimd.dma_start(BT[:], small["bt"]).then_inc(sem("in_late"), 16)
            nc.gpsimd.dma_start(MASK[:], small["mask"]).then_inc(sem("in_late"), 16)
            nc.gpsimd.dma_start(LAMV[:], small["lam"].partition_broadcast(P)).then_inc(sem("in_late"), 16)
        N_SMALL, N_LATE = 10, 6

        @block.tensor
        def _(pe):
            mm = nc.tensor.matmul

            def mod_products(w, pos, v):
                for b in range(2):
                    for k in range(KD):
                        last = mm(PS[MODB][:, pos * 4 + 2 * b:pos * 4 + 2 * b + 2], w[:, k, b * P:(b + 1) * P],
                                  v[:, k, :], start=(k == 0), stop=(k == KD - 1))
                last.then_inc(s_page, 1)

            def mod_group(stage, g=0):
                _, n, _ = MOD_GROUPS[stage]
                if MOD_BEFORE[stage] + g:
                    pe.wait_ge(s_modev, MOD_BEFORE[stage] + g)
                for q in range(n):
                    w = arrived(pe, PA[stage] + g * n + q).rearrange("p (k n) -> p k n", k=KD)
                    mod_products(w, q, CA[:, :, 0:2] if stage[:3] == "ada" else CA[:, :, 1:3])

            def norm(n, src_tiles=KD, name=None):
                ps = opened(pe, f"ss{n}")
                for k in range(KD):
                    if k % 2 == 0:
                        pe.wait_ge(s_sq, NCH * n + k // 2 + 1)
                    last = mm(ps[:, 0:S], ONES[:], XR[:, k, :], start=(k == 0), stop=(k == KD - 1))
                last.then_inc(s_tile, 1)

            def y_ready(n, k=KD - 1):
                pe.wait_ge(s_y, NCH * n + k // 2 + 1)

            def linear(p, ps, x, n=None, k_tiles=KD, width=2, inc=True, wcol=FU, off=0):
                w = arrived(pe, p)[:, 0:k_tiles * wcol].rearrange("p (k n) -> p k n", k=k_tiles)
                for b in range(width):
                    for k in range(k_tiles):
                        if n is not None and b == 0 and k % 2 == 0:
                            y_ready(n, k)
                        last = mm(ps[:, b * S:(b + 1) * S], w[:, k, off + b * P:off + (b + 1) * P], x[:, k, :],
                                  start=(k == 0), stop=(k == k_tiles - 1))
                if inc:
                    last.then_inc(s_page, 1)
                return last

            def ff_pass(name):
                p0, u0, n, mcol, x, routed = PASSES[name]
                acc = {"moe": "acc_moe", "ctx_ff": "acc_ctx", "ff00": "acc_00", "ff01": "acc_01",
                       "ff10": "acc_10", "ff11": "acc_11"}[name]
                for b in range(4):
                    ps = opened(pe, acc, b)
                    mm(ps[:, :], ZW[:], ZX[:], start=True, stop=True, skip_group_check=True)
                for b in (*GU, MISC):
                    rel = last_read[b]
                    if rel is not None:
                        pe.wait_ge(*rel)

                def unit(par, i):
                    p = p0 + UNIT_PAGES * par
                    U = u0 + par
                    if routed:
                        pe.wait_ge(sem("cmask"), i * 2 + (par + 1))
                        mm(PS[MISC][:, par * S:(par + 1) * S], ONES[0:NEXP, :], CMASK[:, par, :],
                           start=True, stop=True, skip_group_check=True)
                    for j in range(2):
                        w = arrived(pe, p + j, i, 16).rearrange("p (k g n) -> p k g n", k=KD, g=2)
                        pe.wait_ge(s_hid, i * 4 + (2 * U + j + 1))
                        for g in range(2):
                            for k in range(KD):
                                last = mm(PS[GU[j]][:, g * S:(g + 1) * S], w[:, k, g, :], x[:, k, :],
                                          start=(k == 0), stop=(k == KD - 1), skip_group_check=True)
                        last.then_inc(s_page, 1)
                    if mcol is not None:
                        mod_page_unit(p + 2, par, i)
                    w = arrived(pe, p + 3, i, 16).rearrange("p (j n) -> p j n", j=2)
                    for j in range(2):
                        pe.wait_ge(s_hid, i * 4 + (2 * U + j + 3))
                        for b in range(KD):
                            last = mm(PS[ACC[b // 2]][:, (b % 2) * S:(b % 2 + 1) * S], w[:, j, b * P:(b + 1) * P],
                                      HID[:, par, j, :], start=False, stop=True, skip_group_check=True)
                            if mcol is None and j == 1 and b == KD - 2:
                                last.then_inc(s_page, 1)
                    last.then_inc(s_page, 1)

                def mod_page_unit(p, par, i):
                    w = arrived(pe, p, i, 16).rearrange("p (k n) -> p k n", k=KD)
                    pe.wait_ge(s_modev, i * 2 + (MOD_BEFORE[name] + par))
                    mod_products(w, 0, CA[:, :, 1:3])

                if n // 2 > 1:
                    with pe.Fori(0, n // 2) as i:
                        unit(0, i)
                        unit(1, i)
                if n % 2:
                    unit(0, n // 2)

            last_read = {}

            def before(name):
                last_read.clear()
                for b in range(8):
                    last_read[b] = None
                for key in order:
                    if key[0] == name:
                        break
                    last_read[tiles[key][0]] = tiles[key][2]

            pe.wait_ge(sem("silu_c"), 1)
            mod_group("ada_a")
            pe.wait_ge(sem("ones"), 1)
            norm(0)
            linear(PA["win_q"], opened(pe, "q"), Y, n=0)
            linear(PA["win_kv"], opened(pe, "kv"), Y)
            pe.wait_ge(sem("in_small"), 16 * N_SMALL)
            ps = opened(pe, "kr")
            for k in range(KD):
                last = mm(ps[NOPE:QKD, 0:S], WKR[:, k, :], Y[:, k, :], start=(k == 0), stop=(k == KD - 1))
            last.then_inc(s_tile, 1)
            for q in range(2):
                linear(PA["win_f"] + q, opened(pe, "f", q), Y)
            ps = opened(pe, "sslat")
            pe.wait_ge(sem("lat_sq"), 1)
            for t in range(2):
                for k in range(KL):
                    last = mm(ps[:, t * S:(t + 1) * S], ONES[:], XR[:, t * KL + k, :], start=(k == 0), stop=(k == KL - 1))
            last.then_inc(s_tile, 1)
            for q in range(8):
                linear(PA["win_g"] + q, opened(pe, "g", q), Y)
            pe.wait_ge(sem("lat_n"), 4)
            w = arrived(pe, PA["uq"])[:, 0:KL * H1 * QKD].rearrange("p (k h n) -> p k h n", k=KL, h=H1)
            for t in range(4):
                ps = opened(pe, f"qh{t}")
                for hh in range(2):
                    for k in range(KL):
                        last = mm(ps[0:QKD, hh * S:(hh + 1) * S], w[:, k, 2 * t + hh, :], QL[:, k, :],
                                  start=(k == 0), stop=(k == KL - 1))
                last.then_inc(s_tile if t < 3 else s_page, 1)
            w = arrived(pe, PA["uk"])[:, 0:KL * H1 * NOPE].rearrange("p (k h n) -> p k h n", k=KL, h=H1)
            for t in range(4):
                ps = opened(pe, f"kh{t}")
                for hh in range(2):
                    for k in range(KL):
                        last = mm(ps[0:NOPE, hh * S:(hh + 1) * S], w[:, k, 2 * t + hh, :], QL[:, KL + k, :],
                                  start=(k == 0), stop=(k == KL - 1))
                last.then_inc(s_tile if t < 3 else s_page, 1)
            w = arrived(pe, PA["uv"])[:, 0:KL * H1 * VD].rearrange("p (k n) -> p k n", k=KL)
            for t in range(TB):
                ps = opened(pe, f"v{t}")
                for k in range(KL):
                    last = mm(ps[:, :], QL[:, KL + k, t * P:(t + 1) * P], w[:, k, :], start=(k == 0), stop=(k == KL - 1))
                last.then_inc(s_tile if t < TB - 1 else s_page, 1)
            pe.wait_ge(s_fa, tiles["qh3", 0][2][1])
            pe.wait_ge(sem("kr_zero"), 1)
            QKf = QK.rearrange("p h t -> p (h t)")
            for t in range(5):
                n = 512 if t < 4 else S
                ps = opened(pe, "rot", t)
                mm(ps[0:QKD, 0:n], ROTA[:], QKf[:, t * 512:t * 512 + n], start=True, stop=True).then_inc(s_tile, 1)

            def scores1(h):
                ps = opened(pe, f"s{h}")
                if h == 0:
                    pe.wait_ge(sem("rope1"), 1)
                for qb in range(TB):
                    last = mm(ps[:, qb * S:(qb + 1) * S], QK[:, h, qb * P:(qb + 1) * P], KH[:, h, :],
                              start=True, stop=True)
                last.then_inc(s_tile, 1)

            def turn1(h):
                ps = opened(pe, f"pt{h}")
                pe.wait_ge(sem("pn1"), h + 1)
                for kb in range(TB):
                    for qb in range(TB):
                        last = nc.tensor.transpose(ps[:, kb * S + qb * P:kb * S + (qb + 1) * P],
                                                   P1[:, h % 2, qb, kb * P:(kb + 1) * P], IDENT[:])
                last.then_inc(s_tile, 1)

            def pv1(h):
                if h % 2 == 0:
                    opened(pe, f"o{h // 2}")
                ps = bank(f"o{h // 2}")
                pe.wait_ge(sem("pt1"), h + 1)
                o = VD * (h % 2)
                for kb in range(TB):
                    last = mm(ps[o:o + VD, 0:S], V1[:, kb, h * VD:(h + 1) * VD], PT1[:, h % 2, kb, :],
                              start=(kb == 0), stop=(kb == TB - 1), skip_group_check=True)
                return last

            for h in range(H1 + 1):
                if h < H1:
                    scores1(h)
                if h >= 1:
                    turn1(h - 1)
                    mod_group("ada_b", h - 1)
                    last = pv1(h - 1)
                    if (h - 1) % 2 == 1:
                        last.then_inc(sem("o1_done"), 1)
            pe.wait_ge(s_fd, tiles["f", 1][2][1])
            for t in range(4):
                tb, fp = t // 2, t % 2
                ps = opened(pe, "fd", t)
                for q in range(2):
                    last = mm(ps[:, q * S:(q + 1) * S], FT[:, 2 * fp + q, tb * P:(tb + 1) * P],
                              DFTD[:].rearrange("p c n -> p (c n)"), start=True, stop=True)
                last.then_inc(s_tile, 1)
            pe.wait_ge(s_fd, tiles["fd", 3][2][1])
            for t in range(2):
                ps = opened(pe, "fs", t)
                for q in range(2):
                    ft = 2 * t + q
                    for c in range(4):
                        last = mm(ps[:, q * S:(q + 1) * S], U2[:, c // 2, c % 2, ft * P:(ft + 1) * P],
                                  DFTS[:, c // 2, c % 2, :], start=(c == 0), stop=(c == 3))
                last.then_inc(s_tile, 1)
            for t, (nm, x) in enumerate((("bra", AT), ("brf", FO))):
                if t == 0:
                    pe.wait_ge(sem("at_done"), 4)
                else:
                    pe.wait_ge(s_fd, tiles["fs", 1][2][1])
                for q in range(4):
                    ps = opened(pe, nm, q)
                    linear(PA["br"] + 2 * t + q // 2, ps, x, k_tiles=4, wcol=512, off=(q % 2) * S, inc=(q % 2 == 1))
            for q in range(4):
                ps = opened(pe, "wout", q)
                if q == 0:
                    pe.wait_ge(sem("merged"), 4)
                linear(PA["wout"] + q, ps, G)
            norm(1)
            mod_group("ada_f")
            y_ready(1)
            ps = opened(pe, "rt")
            for t in range(TB):
                for k in range(KD):
                    last = mm(ps[:, t * 64:t * 64 + NG + NEXP], Y[:, k, t * P:(t + 1) * P], WRT[:, k, :],
                              start=(k == 0), stop=(k == KD - 1))
            last.then_inc(s_tile, 1)
            ps = opened(pe, "ct")
            pe.wait_ge(sem("comb"), 1)
            for t in range(TB):
                last = nc.tensor.transpose(ps[0:NEXP, t * P:(t + 1) * P], RW[:, 7, t * NEXP:(t + 1) * NEXP], IDENT[:])
            last.then_inc(s_tile, 1)
            before("acc_moe")
            ff_pass("moe")
            norm(2)
            mod_group("m0_tail")

            norm(3)
            norm(4)
            y_ready(3)
            before("acc_ctx")
            ff_pass("ctx_ff")
            y_ready(4)
            before("acc_00")
            ff_pass("ff00")
            norm(5)
            norm(6)
            for q in range(2):
                linear(PA["proj"] + q, opened(pe, "qa", q), Y, n=6)
            for q in range(2):
                for c, x in ((0, Y), (1, YC)):
                    linear(PA["proj"] + 2 + q, opened(pe, f"ka{q}", c), x, inc=(c == 1))

            def values(nm, base):
                for q in range(2):
                    w = arrived(pe, base + q).rearrange("p (k n) -> p k n", k=KD)
                    for c, x in ((0, Y), (1, YC)):
                        ps = opened(pe, f"{nm}{q}", c)
                        for t in range(TB):
                            for k in range(KD):
                                last = mm(ps[:, t * S:(t + 1) * S], x[:, k, t * P:(t + 1) * P], w[:, k, :],
                                          start=(k == 0), stop=(k == KD - 1))
                    last.then_inc(s_page, 1)

            values("va", PA["proj"] + 4)
            for q in range(2):
                linear(PA["proj"] + 6 + q, opened(pe, "qb", q), Y)
            for q in range(2):
                for c, x in ((0, Y), (1, YC)):
                    linear(PA["proj"] + 8 + q, opened(pe, f"kb{q}", c), x, inc=(c == 1))
            values("vb", PA["proj"] + 10)
            pe.wait_ge(s_fa, tiles["kb1", 1][2][1])
            pe.wait_ge(sem("in_late"), 16 * N_LATE)
            for t in range(4):
                ps = opened(pe, "rotb", t)
                for q in range(2):
                    x = QB[:, 2 * t + q, :] if t < 2 else KB[:, 2 * (t - 2) + q, 0:S]
                    last = mm(ps[:, q * S:(q + 1) * S], ROTB[:], x, start=True, stop=True)
                last.then_inc(s_tile, 1)

            mod_group("m1_tail")

            def turn2(name, semn, a, src):
                ps = opened(pe, name)
                pe.wait_ge(sem(semn), a + 1)
                for kt in range(NKT):
                    last = nc.tensor.transpose(ps[:, kt * P:(kt + 1) * P], src[:, kt * P:(kt + 1) * P], IDENT[:])
                last.then_inc(s_tile, 1)

            for a in range(NA_N + 1):
                if a < NA_N:
                    h, qb = a // TB, a % TB
                    o = HD * (h % 2)
                    if a == 0:
                        pe.wait_ge(s_fd, tiles["va1", 1][2][1])
                    ps = opened(pe, f"sa{a}")
                    mm(ps[:, :], QA[o:o + HD, h // 2, qb * P:(qb + 1) * P], KA[o:o + HD, h // 2, :],
                       start=True, stop=True).then_inc(s_tile, 1)
                if a >= 1:
                    b = a - 1
                    h, qb = b // TB, b % TB
                    turn2(f"pta{b}", "pn2", b, P2[:, b % 2, 0, :])
                    if qb == 1:
                        if h % 2 == 0:
                            opened(pe, f"oa{h // 2}")
                        ps = bank(f"oa{h // 2}")
                        pe.wait_ge(sem("pt2"), b + 1)
                        o = HD * (h % 2)
                        for kt in range(NKT):
                            last = mm(ps[o:o + HD, 0:S], VA[:, kt, h * HD:(h + 1) * HD], PT2[:, h % 2, kt, :],
                                      start=(kt == 0), stop=(kt == NKT - 1), skip_group_check=True)
                        if h % 2 == 1:
                            last.then_inc(sem("oa_done"), 1)
            for a in range(DF_N + 1):
                if a < DF_N:
                    h, qb = a // TB, a % TB
                    if a == 0:
                        pe.wait_ge(sem("rope2"), 1)
                    for mp in range(2):
                        o = HD * mp
                        ps = opened(pe, f"sd{2 * a + mp}")
                        mm(ps[:, :], QB[o:o + HD, h, qb * P:(qb + 1) * P], KB[o:o + HD, h, :],
                           start=True, stop=True).then_inc(s_tile, 1)
                if a >= 1:
                    b = a - 1
                    h, qb = b // TB, b % TB
                    turn2(f"ptd{b}", "pn3", b, P2[:, b % 2, 0, :])
                    if qb == 1:
                        ps = opened(pe, f"od{h}")
                        pe.wait_ge(sem("pt3"), b + 1)
                        for kt in range(NKT):
                            last = mm(ps[:, 0:S], VB[:, kt, h * P:(h + 1) * P], PT2[:, h % 2, kt, :],
                                      start=(kt == 0), stop=(kt == NKT - 1))
                        last.then_inc(s_tile, 1)
            for t in range(2):
                ps = opened(pe, "sssub", t)
                pe.wait_ge(sem("sub_sq"), t + 1)
                mm(ps[:, :], ONES[:], XR[:, 2 * t:2 * t + 2, :].rearrange("p a t -> p (a t)"),
                   start=True, stop=True).then_inc(s_tile, 1)
            for q in range(4):
                ps = opened(pe, "aout", q)
                if q == 0:
                    pe.wait_ge(sem("sub_done"), 1)
                linear(PA["aout"] + q, ps, MG)
            norm(7)
            y_ready(7)
            before("acc_01")
            ff_pass("ff01")
            norm(8)
            y_ready(8)
            before("acc_10")
            ff_pass("ff10")
            norm(9)
            for q in range(4):
                linear(PA["cin"] + 2 * q, opened(pe, f"cg{q}"), Y, n=9)
                linear(PA["cin"] + 2 * q + 1, opened(pe, f"ch{q}"), Y)
            for q in range(4):
                linear(PA["cin"] + 8 + q, opened(pe, "cb", q), Y)
            for q in range(4):
                ps = opened(pe, "cout", q)
                if q == 0:
                    pe.wait_ge(sem("bv_done"), 8)
                linear(PA["cout"] + q, ps, BV)
            norm(10)
            y_ready(10)
            before("acc_11")
            ff_pass("ff11")
            norm(11)

        @block.scalar
        def _(act):
            f = nc.scalar.activation
            chain = [0]

            def link(ins):
                chain[0] += 1
                ins.then_inc(s_ac, 1)
                act.wait_ge(s_ac, chain[0])

            def free(ins, name, i=0):
                assert tiles[name, i][2][0] is s_fa or tiles[name, i][2][0] == s_fa
                ins.then_inc(s_fa, 1)

            def norm(n, src_ready=None):
                src, dst, _, _, sc, sh, _ = NORMS[n]
                if n:
                    act.wait_ge(s_y, NCH * n)
                for c in range(NCH):
                    if src_ready is not None:
                        src_ready(c)
                    f(XR[:, 2 * c:2 * c + 2, :], src[:, 2 * c:2 * c + 2, :], ACT.Square).then_inc(s_sq, 1)
                ps = filled(act, f"ss{n}")
                free(f(RT[:, 0:S], ps[:, 0:S], ACT.Sqrt, bias=EPSC[:, 0:1], scale=1.0 / D), f"ss{n}")
                act.wait_ge(s_ri, n + 1)
                for c in range(NCH):
                    act.wait_ge(s_xr, NCH * n + c + 1)
                    for k in (2 * c, 2 * c + 1):
                        if sh is None:
                            last = f(dst[:, k, :], XR[:, k, :], ACT.Copy, scale=NA_[:, k:k + 1])
                        else:
                            last = f(dst[:, k, :], XR[:, k, :], ACT.Identity, scale=NA_[:, k:k + 1],
                                     bias=MODT[:, sh + k, NORMS[n][6]:NORMS[n][6] + 1])
                    last.then_inc(s_y, 1)

            def ff_pass(name):
                p0, u0, n, mcol, x, routed = PASSES[name]

                def unit(par, i):
                    for j in range(2):
                        act.wait_ge(s_page, i * 8 + (p0 + UNIT_PAGES * par + j + 1))
                        f(SIL[:, j, :], PS[GU[j]][:, 0:S], ACT.Silu).then_inc(s_silu, 1)

                if n // 2 > 1:
                    with act.Fori(0, n // 2) as i:
                        unit(0, i)
                        unit(1, i)
                if n % 2:
                    unit(0, n // 2)

            def soft_exp(out, ps, bias, total):
                return f(out, ps, ACT.Exp, bias=bias, accum_out=total)

            act.wait_ge(sem("in_vecs"), 16)
            f(CA[:].rearrange("p k v -> p v k"), V[:, VCOL["c"]:VCOL["c"] + 24].rearrange("p (v k) -> p v k", v=3),
              ACT.Silu).then_inc(sem("silu_c"), 1)
            act.wait_ge(sem("eps"), 1)
            act.wait_ge(sem("in_x"), 16)
            norm(0)
            ps = filled(act, "q")
            free(f(QL[:, 0:KL, :], ps[:, :].rearrange("p (a t) -> p a t", a=2), ACT.Copy), "q")
            ps = filled(act, "kv")
            free(f(QL[:, KL:2 * KL, :], ps[:, :].rearrange("p (a t) -> p a t", a=2), ACT.Copy), "kv")
            ps = filled(act, "kr")
            free(f(QK[NOPE:QKD, 8, :], ps[NOPE:QKD, 0:S], ACT.Copy), "kr")
            act.wait_ge(s_fa, tiles["kv", 0][2][1])
            f(XR[:, 0:4, :], QL[:, :, :], ACT.Square).then_inc(sem("lat_sq"), 1)
            ps = filled(act, "sslat")
            free(f(RT[:, :], ps[:, :], ACT.Sqrt, bias=EPSC[:, 0:1], scale=1.0 / LORA), "sslat")
            act.wait_ge(sem("ang"), 1)
            f(CSA[:], ANG[:], ACT.Sin).then_inc(sem("csa"), 1)
            for q in range(8):
                ps = filled(act, "g", q)
                for b in range(2):
                    j = 2 * q + b
                    last = f(G[:, j, :], ps[:, b * S:(b + 1) * S], ACT.Sigmoid,
                             bias=V[:, VCOL["b_gates"] + j:VCOL["b_gates"] + j + 1])
                free(last, "g", q)
            for t in range(4):
                ps = filled(act, f"qh{t}")
                free(f(QK[:, 2 * t:2 * t + 2, :], ps[0:QKD, :].rearrange("p (a t) -> p a t", a=2), ACT.Copy,
                       scale=float(QKD) ** -0.5), f"qh{t}")

            def exp1(h):
                act.wait_ge(sem("mx1"), h + 1)
                ps = bank(f"s{h}")
                for qb in range(TB):
                    c = 4 * (h % 2) + qb
                    last = soft_exp(P1[:, h % 2, qb, :], ps[:, qb * S:(qb + 1) * S], ST[:, c:c + 1], ST[:, c + 2:c + 3])
                last.then_inc(sem("exp1"), 1)

            def copy1(h):
                ps = filled(act, f"pt{h}")
                f(PT1[:, h % 2, :, :], ps[:, :].rearrange("p (a t) -> p a t", a=2), ACT.Copy).then_inc(sem("pt1"), 1)

            for h in range(H1 + 1):
                if h < H1:
                    exp1(h)
                if h >= 1:
                    copy1(h - 1)
            norm(1, lambda c: act.wait_ge(s_fd, tiles["wout", c][2][1]))
            act.wait_ge(sem("rt_gd"), 1)
            link(f(RW[:, 1, 0:8], RW[:, 1, 0:8], ACT.Exp))
            act.wait_ge(sem("rt_d2"), 1)
            f(RW[:, 1, 8:10], RW[:, 1, 8:10], ACT.Exp).then_inc(sem("rt_exp"), 1)
            ff_pass("moe")
            norm(2, lambda c: act.wait_ge(s_fd, tiles["acc_moe", c][2][1]))
            act.wait_ge(sem("in_late"), 16 * N_LATE)
            norm(3)
            norm(4)
            ff_pass("ctx_ff")
            ff_pass("ff00")
            norm(5, lambda c: act.wait_ge(s_fd, tiles["acc_ctx", c][2][1]))
            norm(6, lambda c: act.wait_ge(s_fd, tiles["acc_00", c][2][1]))

            def two(ps):
                return ps[:, :].rearrange("p (a t) -> p a t", a=2)

            for q in range(2):
                free(f(QA[:, 2 * q:2 * q + 2, :], two(filled(act, "qa", q)), ACT.Copy, scale=HD ** -0.5), "qa", q)
            for q in range(2):
                for c in range(2):
                    free(f(KA[:, 2 * q:2 * q + 2, c * S:(c + 1) * S], two(filled(act, f"ka{q}", c)), ACT.Copy), f"ka{q}", c)
            for q in range(2):
                free(f(QB[:, 2 * q:2 * q + 2, :], two(filled(act, "qb", q)), ACT.Copy, scale=HD ** -0.5), "qb", q)
            for q in range(2):
                for c in range(2):
                    free(f(KB[:, 2 * q:2 * q + 2, c * S:(c + 1) * S], two(filled(act, f"kb{q}", c)), ACT.Copy), f"kb{q}", c)
            act.wait_ge(sem("lam_dot"), 1)
            f(LAMT[:, 2:4], LAMT[:, 0:2], ACT.Exp).then_inc(sem("lam_exp"), 1)
            for a in range(NA_N + 1):
                if a < NA_N:
                    act.wait_ge(sem("mx2"), a + 1)
                    c = 4 * (a % 2)
                    soft_exp(P2[:, a % 2, 0, :], bank(f"sa{a}")[:, :], ST[:, c:c + 1], ST[:, c + 2:c + 3])\
                        .then_inc(sem("exp2"), 1)
                if a >= 1:
                    b = a - 1
                    ps = filled(act, f"pta{b}")
                    h, qb = b // TB, b % TB
                    f(PT2[:, h % 2, :, qb * P:(qb + 1) * P], ps[:, :].rearrange("p (a t) -> p a t", a=NKT), ACT.Copy)\
                        .then_inc(sem("pt2"), 1)
            for a in range(DF_N + 1):
                if a < DF_N:
                    for mp in range(2):
                        act.wait_ge(sem("mx3"), 2 * a + mp + 1)
                        c = 4 * (a % 2) + mp
                        soft_exp(P2[:, a % 2, mp, :], bank(f"sd{2 * a + mp}")[:, :], ST[:, c:c + 1], ST[:, c + 2:c + 3])\
                            .then_inc(sem("exp3"), 1)
                if a >= 1:
                    b = a - 1
                    ps = filled(act, f"ptd{b}")
                    h, qb = b // TB, b % TB
                    f(PT2[:, h % 2, :, qb * P:(qb + 1) * P], ps[:, :].rearrange("p (a t) -> p a t", a=NKT), ACT.Copy)\
                        .then_inc(sem("pt3"), 1)
            for t in range(2):
                act.wait_ge(s_fd, tiles[f"od{2 * t + 1}", 0][2][1])
                f(XR[:, 2 * t:2 * t + 2, :], MG[:, 4 + 2 * t:6 + 2 * t, :], ACT.Square).then_inc(sem("sub_sq"), 1)
            for t in range(2):
                ps = filled(act, "sssub", t)
                if t == 1:
                    act.wait_ge(sem("sub_ri"), 1)
                free(f(RT[:, :], ps[:, :], ACT.Sqrt, bias=EPSC[:, 0:1], scale=1.0 / P), "sssub", t)
            norm(7, lambda c: act.wait_ge(s_fd, tiles["aout", c][2][1]))
            ff_pass("ff01")
            norm(8, lambda c: act.wait_ge(s_fd, tiles["acc_01", c][2][1]))
            ff_pass("ff10")
            norm(9, lambda c: act.wait_ge(s_fd, tiles["acc_10", c][2][1]))
            for q in range(4):
                free(f(CG[:, 2 * q:2 * q + 2, :], two(filled(act, f"cg{q}")), ACT.Copy), f"cg{q}")
            norm(10, lambda c: act.wait_ge(s_fd, tiles["cout", c][2][1]))
            ff_pass("ff11")
            norm(11, lambda c: act.wait_ge(s_fd, tiles["acc_11", c][2][1]))
            act.wait_ge(s_y, NCH * 12)
            act.dma_start(small["out"], Y[:]).then_inc(sem("stored"), 16)
            act.wait_ge(sem("stored"), 16)

        @block.vector
        def _(dve):
            v = nc.vector
            chain = [0]

            def link(ins):
                chain[0] += 1
                ins.then_inc(s_dc, 1)
                dve.wait_ge(s_dc, chain[0])

            def free(ins, name, i=0):
                assert tiles[name, i][2][0] == s_fd
                ins.then_inc(s_fd, 1)

            def vec(name, k, n=1):
                return V[:, VCOL[name] + k:VCOL[name] + k + n]

            def two(ps):
                return ps[:, :].rearrange("p (a t) -> p a t", a=2)

            def mod_take(stage, g=0):
                col, n, _ = MOD_GROUPS[stage]
                col += 2 * n * g
                dve.wait_ge(s_page, PA[stage] + n * (g + 1))
                v.tensor_tensor(MODT[:, col:col + 2 * n, :],
                                PS[MODB][:, 0:4 * n].rearrange("p (b v) -> p b v", v=2),
                                MB[:, col:col + 2 * n, :], ALU.add).then_inc(s_modev, 1)

            def mods_taken(stage):
                dve.wait_ge(s_modev, MOD_BEFORE[stage] + MOD_GROUPS[stage][2])

            def norm(n):
                src, dst, gname, goff, sc, sh, vi = NORMS[n]
                dve.wait_ge(s_y, NCH * n) if n else None
                if sc is None:
                    v.tensor_copy(NA_[:], vec(gname, goff, KD)).then_inc(sem("norm_gain"), 1)
                else:
                    v.scalar_tensor_tensor(out=NA_[:], in0=MODT[:, sc:sc + KD, vi], scalar=1.0,
                                           in1=vec(gname, goff, KD), op0=ALU.add, op1=ALU.mult)\
                        .then_inc(sem("norm_gain"), 1)
                dve.wait_ge(sem("norm_gain"), n + 1)
                dve.wait_ge(*tiles[f"ss{n}", 0][2])
                v.reciprocal(RI[:, 0:S], RT[:, 0:S]).then_inc(s_ri, 1)
                dve.wait_ge(s_ri, n + 1)
                for c in range(NCH):
                    v.tensor_tensor(XR[:, 2 * c:2 * c + 2, :], src[:, 2 * c:2 * c + 2, :],
                                    RI[:, 0:S].unsqueeze(1).broadcast_to([P, 2, S]), ALU.mult).then_inc(s_xr, 1)

            def residual(name, coef):
                dst, col = coef
                for q in range(4):
                    ps = filled(dve, name, q)
                    for b in range(2):
                        k = 2 * q + b
                        last = v.scalar_tensor_tensor(out=dst[:, k, :], in0=ps[:, b * S:(b + 1) * S], scalar=col(k),
                                                      in1=dst[:, k, :], op0=ALU.mult, op1=ALU.add)
                    free(last, name, q)

            def modcol(c, vi=0):
                return lambda k: MODT[:, c + k, vi:vi + 1]

            def half_gate(c, vi=0):
                link(v.tensor_scalar(HG[:], MODT[:, c:c + KD, vi], 0.5, None, ALU.mult))
                return lambda k: HG[:, k:k + 1]

            def ff_pass(name):
                p0, u0, n, mcol, x, routed = PASSES[name]

                def mask(par, e):
                    v.tensor_scalar(CMASK[:, par, :], COMBT[:], IDENT[0:NEXP, bass.ds(e, 1)], None, ALU.mult)\
                        .then_inc(sem("cmask"), 1)

                if routed:
                    mask(0, 0)

                def unit(par, i):
                    U = u0 + par
                    if routed:
                        mask(1 - par, i * 2 + (par + 1))
                    for j in range(2):
                        dve.wait_ge(s_silu, i * 4 + (2 * U + j + 1))
                        up = PS[GU[j]][:, S:2 * S]
                        if routed:
                            v.tensor_tensor(TG[:, j, :], up, SIL[:, j, :], ALU.mult).then_inc(sem("tg"), 1)
                            dve.wait_ge(sem("tg"), i * 4 + (2 * par + j + 1))
                            v.tensor_tensor(HID[:, par, j, :], PS[MISC][:, par * S:(par + 1) * S], TG[:, j, :],
                                            ALU.mult).then_inc(s_hid, 1)
                        else:
                            v.tensor_tensor(HID[:, par, j, :], up, SIL[:, j, :], ALU.mult).then_inc(s_hid, 1)
                    if mcol is not None:
                        dve.wait_ge(s_page, i * 8 + (p0 + UNIT_PAGES * par + 3))
                        v.tensor_tensor(MODT[:, bass.ds(i * 4 + (mcol + 2 * par), 2), :],
                                        PS[MODB][:, 0:4].rearrange("p (b v) -> p b v", b=2),
                                        MB[:, bass.ds(i * 4 + (mcol + 2 * par), 2), :], ALU.add).then_inc(s_modev, 1)

                if n // 2 > 1:
                    with dve.Fori(0, n // 2) as i:
                        unit(0, i)
                        unit(1, i)
                if n % 2:
                    unit(0, n // 2)

            v.memset(EPSC[:], EPS).then_inc(sem("eps"), 1)
            v.memset(ZW[:], 0.0)
            v.memset(ZX[:], 0.0)
            v.memset(HID[:, 0, :, :], 0.0).then_inc(s_hid, 1)
            v.memset(HID[:, 1, :, :], 0.0).then_inc(s_hid, 1)
            v.memset(ONES[:], 1.0).then_inc(sem("ones"), 1)
            v.memset(QK[0:NOPE, 8, :], 0.0).then_inc(sem("kr_zero"), 1)
            dve.wait_ge(sem("in_mb"), 16)
            dve.wait_ge(sem("in_vecs"), 16)
            dve.wait_ge(sem("in_small"), 16 * N_SMALL)
            link(v.tensor_copy(AK[:, 0, :], POSI[:]))
            link(v.tensor_scalar(ANG[:, 0, :], AK[:, 0, :], INVF[:, 0:1], None, ALU.mult))
            link(v.tensor_copy(ANG[:, 1, :], ANG[:, 0, :]))
            MAGIC = 1.5 * 2.0 ** 23
            link(v.tensor_scalar(AK[:, 0, :], ANG[:, 0, :], 1.0 / (2.0 * np.pi), 0.25, ALU.mult, ALU.add))
            link(v.tensor_scalar(AK[:, 1, :], ANG[:, 1, :], 1.0 / (2.0 * np.pi), None, ALU.mult))
            link(v.tensor_scalar(AK[:], AK[:], MAGIC, None, ALU.add))
            link(v.tensor_scalar(AK[:], AK[:], MAGIC, None, ALU.subtract))
            two_pi = 2.0 * np.pi
            parts = []
            rest = two_pi
            for scale in (2.0 ** 5, 2.0 ** 13, 2.0 ** 21):
                part = np.round(rest * scale) / scale
                parts.append(float(part))
                rest -= part
            parts.append(float(np.float32(rest)))
            for part in parts:
                link(v.scalar_tensor_tensor(out=ANG[:], in0=AK[:], scalar=-part, in1=ANG[:], op0=ALU.mult, op1=ALU.add))
            link(v.tensor_scalar(ANG[:, 0, :], ANG[:, 0, :], float(np.pi / 2), None, ALU.add))
            PI = float(np.nextafter(np.float32(np.pi), np.float32(0)))
            v.tensor_scalar(ANG[:], ANG[:], PI, -PI, ALU.min, ALU.max).then_inc(sem("ang"), 1)

            mod_take("ada_a")
            mods_taken("ada_a")
            norm(0)
            for q in range(2):
                free(v.tensor_copy(FT[:, 2 * q:2 * q + 2, :], two(filled(dve, "f", q))), "f", q)
            dve.wait_ge(*tiles["sslat", 0][2])
            link(v.reciprocal(RI[:], RT[:]))
            for t in range(4):
                g = vec("g_q", t) if t < KL else vec("g_kv", t - KL)
                o = (t // KL) * S
                v.scalar_tensor_tensor(out=QL[:, t, :], in0=QL[:, t, :], scalar=g, in1=RI[:, o:o + S],
                                       op0=ALU.mult, op1=ALU.mult).then_inc(sem("lat_n"), 1)
            for t in range(4):
                ps = filled(dve, f"kh{t}")
                free(v.tensor_copy(KH[0:NOPE, 2 * t:2 * t + 2, :], ps[0:NOPE, :].rearrange("p (a t) -> p a t", a=2)), f"kh{t}")
            for t in range(TB):
                free(v.tensor_copy(V1[:, t, :], filled(dve, f"v{t}")[:, :]), f"v{t}")
            dve.wait_ge(sem("csa"), 1)
            filled(dve, "rot", 4)
            link(v.tensor_tensor(QK[:], QK[:], CSA[:, 0:1, :].broadcast_to([QKD, 9, S]), ALU.mult))
            for t in range(5):
                w = 2 if t < 4 else 1
                ps = bank("rot", t)[0:QKD, 0:w * S].rearrange("p (a t) -> p a t", a=w)
                tmp = XR[0:QKD, 0:w, :]
                link(v.tensor_tensor(tmp, ps, CSA[:, 1:2, :].broadcast_to([QKD, w, S]), ALU.mult))
                free(v.tensor_tensor(QK[:, 2 * t:2 * t + w, :], QK[:, 2 * t:2 * t + w, :], tmp, ALU.add), "rot", t)
                dve.wait_ge(*tiles["rot", t][2])
            v.tensor_copy(KH[NOPE:QKD, :, :], QK[NOPE:QKD, 8:9, :].broadcast_to([ROPE, H1, S])).then_inc(sem("rope1"), 1)

            def max1(h):
                ps = filled(dve, f"s{h}")
                c = 4 * (h % 2)
                v.tensor_reduce(ST[:, c:c + 2], two(ps), AX.X, ALU.max, negate=True).then_inc(sem("mx1"), 1)

            def norm1(h):
                c = 4 * (h % 2)
                dve.wait_ge(sem("exp1"), h + 1)
                link(v.reciprocal(ST[:, c + 2:c + 4], ST[:, c + 2:c + 4]))
                v.tensor_tensor(P1[:, h % 2, :, :], P1[:, h % 2, :, :],
                                ST[:, c + 2:c + 4].unsqueeze(2).broadcast_to([P, TB, S]), ALU.mult)\
                    .then_inc(sem("pn1"), 1)

            for h in range(H1 + 2):
                if h < H1:
                    max1(h)
                if 1 <= h <= H1:
                    norm1(h - 1)
                if h >= 2:
                    mod_take("ada_b", h - 2)
                    if (h - 2) % 2 == 1:
                        pr = (h - 2) // 2
                        free(v.tensor_copy(AT[:, pr, :], filled(dve, f"o{pr}")[:, 0:S]), f"o{pr}")
            dve.wait_ge(s_fd, tiles["o3", 0][2][1])
            v.memset(ST[:, 31:32], 0.0).then_inc(sem("at_done"), 4)
            for t in range(4):
                tb, fp = t // 2, t % 2
                ps = filled(dve, "fd", t)
                free(v.tensor_copy(U2[:, tb, :, fp * S:(fp + 1) * S].rearrange("p c (q n) -> p q c n", q=2),
                                   ps[:, :].rearrange("p (q c n) -> p q c n", q=2, c=2)), "fd", t)
            for t in range(2):
                free(v.tensor_copy(FO[:, 2 * t:2 * t + 2, :], two(filled(dve, "fs", t))), "fs", t)
            dve.wait_ge(s_fa, tiles["g", 7][2][1])
            for q in range(4):
                ps = filled(dve, "bra", q)
                free(v.tensor_tensor(G[:, 2 * q:2 * q + 2, :], two(ps), G[:, 2 * q:2 * q + 2, :], ALU.mult), "bra", q)
            for q in range(4):
                ps = filled(dve, "brf", q)
                free(v.tensor_tensor(G[:, 8 + 2 * q:10 + 2 * q, :], two(ps), G[:, 8 + 2 * q:10 + 2 * q, :], ALU.mult), "brf", q)
            for q in range(4):
                dve.wait_ge(*tiles["brf", q][2])
                v.tensor_tensor(G[:, 2 * q:2 * q + 2, :], G[:, 2 * q:2 * q + 2, :], G[:, 8 + 2 * q:10 + 2 * q, :], ALU.add)\
                    .then_inc(sem("merged"), 1)
            mods_taken("ada_b")
            residual("wout", (HT, modcol(ADA + 16)))
            norm(1)
            mod_take("ada_f")

            LG = RW[:, 0, 0:2 * 36].rearrange("p (t n) -> p t n", t=TB)

            def rw(i, *dims, off=0):
                n = int(np.prod(dims))
                a = RW[:, i, off:off + n]
                if len(dims) == 2:
                    return a.rearrange("p (a b) -> p a b", a=dims[0])
                if len(dims) == 3:
                    return a.rearrange("p (a b c) -> p a b c", a=dims[0], b=dims[1])
                return a

            def over(x, n):
                return x.unsqueeze(2).broadcast_to([P, TB, n])

            ps = filled(dve, "rt")
            free(v.tensor_tensor(LG, ps[:, 0:TB * 64].rearrange("p (t n) -> p t n", t=TB)[:, :, 0:36],
                                 BRT[:].unsqueeze(1).broadcast_to([P, TB, 36]), ALU.add), "rt")
            dve.wait_ge(*tiles["rt", 0][2])
            ge = rw(1, TB, NG)
            gm, gs = RW[:, 6, 0:2], RW[:, 6, 2:4]
            eq = rw(2, TB, NG)
            oh = rw(3, TB, NG)
            rev4 = REV[:, 4:8].unsqueeze(1).broadcast_to([P, TB, NG])
            rev8 = REV[:].unsqueeze(1).broadcast_to([P, TB, NE8])
            link(v.tensor_reduce(gm, LG[:, :, 0:NG], AX.X, ALU.max))
            link(v.tensor_tensor(ge, LG[:, :, 0:NG], over(gm, NG), ALU.subtract))
            link(v.scalar_tensor_tensor(out=eq, in0=ge, scalar=0.0, in1=rev4, op0=ALU.is_ge, op1=ALU.mult))
            link(v.tensor_reduce(gs, eq, AX.X, ALU.max))
            v.tensor_tensor(oh, eq, over(gs, NG), ALU.is_equal).then_inc(sem("rt_gd"), 1)
            dve.wait_ge(sem("rt_gd"), 1)
            big = rw(4, TB, NG, NE8)
            link(v.tensor_tensor(big, LG[:, :, NG:].rearrange("p t (g e) -> p t g e", g=NG),
                                 oh.unsqueeze(3).broadcast_to([P, TB, NG, NE8]), ALU.mult))
            el = rw(5, TB, NE8)
            link(v.tensor_reduce(el, big.rearrange("p t g e -> p t e g"), AX.X, ALU.add))
            m1, pm = RW[:, 6, 4:6], RW[:, 6, 6:8]
            d1, oh1, oh2 = rw(2, TB, NE8, off=16), rw(3, TB, NE8, off=16), rw(3, TB, NE8, off=32)
            link(v.tensor_reduce(m1, el, AX.X, ALU.max))
            link(v.tensor_tensor(d1, el, over(m1, NE8), ALU.is_equal))
            link(v.tensor_tensor(d1, d1, rev8, ALU.mult))
            link(v.tensor_reduce(pm, d1, AX.X, ALU.max))
            link(v.tensor_tensor(oh1, d1, over(pm, NE8), ALU.is_equal))
            link(v.scalar_tensor_tensor(out=el, in0=oh1, scalar=NEG, in1=el, op0=ALU.mult, op1=ALU.add))
            m2 = RW[:, 6, 8:10]
            link(v.tensor_reduce(m2, el, AX.X, ALU.max))
            link(v.tensor_tensor(d1, el, over(m2, NE8), ALU.is_equal))
            link(v.tensor_tensor(d1, d1, rev8, ALU.mult))
            link(v.tensor_reduce(pm, d1, AX.X, ALU.max))
            link(v.tensor_tensor(oh2, d1, over(pm, NE8), ALU.is_equal))
            v.tensor_tensor(RW[:, 1, 8:10], m2, m1, ALU.subtract).then_inc(sem("rt_d2"), 1)
            dve.wait_ge(sem("rt_exp"), 1)
            w1, w2, gp = RW[:, 6, 10:12], RW[:, 6, 12:14], RW[:, 6, 14:16]
            link(v.tensor_reduce(gp, ge, AX.X, ALU.add))
            link(v.reciprocal(gp, gp))
            link(v.tensor_scalar(w1, RW[:, 1, 8:10], 1.0, None, ALU.add))
            link(v.reciprocal(w1, w1))
            link(v.tensor_tensor(w2, w1, RW[:, 1, 8:10], ALU.mult))
            link(v.tensor_tensor(w1, w1, gp, ALU.mult))
            link(v.tensor_tensor(w2, w2, gp, ALU.mult))
            link(v.tensor_tensor(oh1, oh1, over(w1, NE8), ALU.mult))
            link(v.tensor_tensor(oh2, oh2, over(w2, NE8), ALU.mult))
            link(v.tensor_tensor(oh1, oh1, oh2, ALU.add))
            for t in range(TB):
                cw = RW[:, 7, t * NEXP:(t + 1) * NEXP].rearrange("p (g e) -> p g e", g=NG)
                last = v.tensor_tensor(cw, oh[:, t, :].unsqueeze(2).broadcast_to([P, NG, NE8]),
                                       oh1[:, t:t + 1, :].broadcast_to([P, NG, NE8]), ALU.mult)
                if t == 0:
                    link(last)
            last.then_inc(sem("comb"), 1)
            free(v.tensor_copy(COMBT[:], filled(dve, "ct")[0:NEXP, 0:S]), "ct")
            dve.wait_ge(*tiles["ct", 0][2])
            ff_pass("moe")
            residual("acc_moe", (HT, modcol(ADA + 40)))
            norm(2)
            mod_take("m0_tail")
            mods_taken("m0_tail")

            dve.wait_ge(sem("in_late"), 16 * N_LATE)
            for h in range(NA_H):
                last = v.tensor_tensor(BT[:, h, :, :], BT[:, h, :, :], MASK[:].unsqueeze(1).broadcast_to([P, 6, GRID]), ALU.add)
            last.then_inc(sem("bias"), 1)
            norm(3)
            norm(4)
            ff_pass("ctx_ff")
            residual("acc_ctx", (CT, half_gate(MOD0 + 16, 1)))
            ff_pass("ff00")
            residual("acc_00", (HT, half_gate(MOD0 + 16, 0)))
            norm(5)
            norm(6)
            for t in range(2):
                link(v.tensor_tensor(LAMV[:, 2 * t, :], LAMV[:, 2 * t, :], LAMV[:, 2 * t + 1, :], ALU.mult))
            v.tensor_reduce(LAMT[:, 0:2], LAMV[:, 0:4:2, :], AX.X, ALU.add).then_inc(sem("lam_dot"), 1)
            for q in range(2):
                for c in range(2):
                    ps = filled(dve, f"va{q}", c)
                    free(v.tensor_copy(VA[:, 2 * c:2 * c + 2, q * S:(q + 1) * S], two(ps)), f"va{q}", c)
            dve.wait_ge(sem("lam_exp"), 1)
            link(v.tensor_tensor(LAMT[:, 4:5], LAMT[:, 2:3], LAMT[:, 3:4], ALU.subtract))
            link(v.tensor_scalar(LAMT[:, 4:5], LAMT[:, 4:5], LAM_INIT, None, ALU.add))
            link(v.tensor_scalar(LAMT[:, 5:6], vec("subln", 0), 1.0 - LAM_INIT, None, ALU.mult))
            for q in range(2):
                for c in range(2):
                    ps = filled(dve, f"vb{q}", c)
                    free(v.tensor_copy(VB[:, 2 * c:2 * c + 2, q * S:(q + 1) * S], two(ps)), f"vb{q}", c)
            for t in range(4):
                ps = filled(dve, "rotb", t)
                x = QB[:, 2 * t:2 * t + 2, :] if t < 2 else KB[:, 2 * (t - 2):2 * (t - 2) + 2, 0:S]
                link(v.tensor_tensor(x, x, CSB[:, 0:1, :].broadcast_to([P, 2, S]), ALU.mult))
                link(v.tensor_tensor(XR[:, 0:2, :], two(ps), CSB[:, 1:2, :].broadcast_to([P, 2, S]), ALU.mult))
                free(v.tensor_tensor(x, x, XR[:, 0:2, :], ALU.add), "rotb", t)
                dve.wait_ge(*tiles["rotb", t][2])
            v.memset(ST[:, 31:32], 0.0).then_inc(sem("rope2"), 1)
            mod_take("m1_tail")
            dve.wait_ge(sem("bias"), 1)

            def maxa(a):
                h, qb = a // TB, a % TB
                ps = filled(dve, f"sa{a}")
                c = 4 * (a % 2)
                link(v.tensor_tensor(ps[:, 0:S].rearrange("p (r c) -> p r c", c=GRID),
                                     ps[:, 0:S].rearrange("p (r c) -> p r c", c=GRID),
                                     BT[:, h, 2 - 2 * qb:6 - 2 * qb, :], ALU.add))
                v.tensor_reduce(ST[:, c:c + 1], ps[:, :], AX.X, ALU.max, negate=True).then_inc(sem("mx2"), 1)

            def norma(a):
                c = 4 * (a % 2)
                dve.wait_ge(sem("exp2"), a + 1)
                link(v.reciprocal(ST[:, c + 2:c + 3], ST[:, c + 2:c + 3]))
                v.tensor_scalar(P2[:, a % 2, 0, :], P2[:, a % 2, 0, :], ST[:, c + 2:c + 3], None, ALU.mult)\
                    .then_inc(sem("pn2"), 1)

            for a in range(NA_N + 2):
                if a < NA_N:
                    maxa(a)
                if 1 <= a <= NA_N:
                    norma(a - 1)
                if a >= 2 and (a - 2) % 4 == 3:
                    pr = (a - 2) // 4
                    free(v.tensor_copy(MG[:, pr, :], filled(dve, f"oa{pr}")[:, 0:S]), f"oa{pr}")

            def maxd(a):
                for mp in range(2):
                    ps = filled(dve, f"sd{2 * a + mp}")
                    c = 4 * (a % 2) + mp
                    v.tensor_reduce(ST[:, c:c + 1], ps[:, :], AX.X, ALU.max, negate=True).then_inc(sem("mx3"), 1)

            def normd(a):
                c = 4 * (a % 2)
                dve.wait_ge(sem("exp3"), 2 * a + 2)
                link(v.reciprocal(ST[:, c + 2:c + 4], ST[:, c + 2:c + 4]))
                link(v.tensor_tensor(ST[:, c + 3:c + 4], ST[:, c + 3:c + 4], LAMT[:, 4:5], ALU.mult))
                link(v.tensor_scalar(P2[:, a % 2, 1, :], P2[:, a % 2, 1, :], ST[:, c + 3:c + 4], None, ALU.mult))
                v.scalar_tensor_tensor(out=P2[:, a % 2, 0, :], in0=P2[:, a % 2, 0, :], scalar=ST[:, c + 2:c + 3],
                                       in1=P2[:, a % 2, 1, :], op0=ALU.mult, op1=ALU.subtract)\
                    .then_inc(sem("pn3"), 1)

            for a in range(DF_N + 2):
                if a < DF_N:
                    maxd(a)
                if 1 <= a <= DF_N:
                    normd(a - 1)
                if a >= 2 and (a - 2) % 2 == 1:
                    h = (a - 2) // 2
                    free(v.tensor_copy(MG[:, 4 + h, :], filled(dve, f"od{h}")[:, 0:S]), f"od{h}")
            for t in range(2):
                dve.wait_ge(*tiles["sssub", t][2])
                ri = v.reciprocal(RI[:], RT[:]).then_inc(sem("sub_ri"), 1)
                dve.wait_ge(sem("sub_ri"), t + 1)
                link(v.scalar_tensor_tensor(out=MG[:, 4 + 2 * t:6 + 2 * t, :], in0=MG[:, 4 + 2 * t:6 + 2 * t, :],
                                            scalar=LAMT[:, 5:6], in1=RI[:].rearrange("p (a t) -> p a t", a=2),
                                            op0=ALU.mult, op1=ALU.mult))
            v.memset(ST[:, 31:32], 0.0).then_inc(sem("sub_done"), 1)
            residual("aout", (HT, modcol(MOD0 + 40)))
            norm(7)
            ff_pass("ff01")
            residual("acc_01", (HT, half_gate(MOD0 + 64, 0)))
            norm(8)
            ff_pass("ff10")
            residual("acc_10", (HT, half_gate(MOD1 + 16, 0)))
            norm(9)
            link(v.memset(UU[:, :, 0:1], 0.0))
            link(v.memset(UU[:, :, S + 1:S + 2], 0.0))
            for q in range(4):
                ps = filled(dve, f"ch{q}")
                dve.wait_ge(*tiles[f"cg{q}", 0][2])
                free(v.tensor_tensor(UU[:, 2 * q:2 * q + 2, 1:S + 1], two(ps), CG[:, 2 * q:2 * q + 2, :], ALU.mult), f"ch{q}")
            dve.wait_ge(*tiles["ch3", 0][2])
            for tap in range(3):
                for k in range(KD):
                    w = vec("conv_w", 8 * tap + k)
                    if tap == 0:
                        last = v.tensor_scalar(VV[:, k, :], UU[:, k, 0:S], w, None, ALU.mult)
                    else:
                        last = v.scalar_tensor_tensor(out=VV[:, k, :], in0=UU[:, k, tap:tap + S], scalar=w,
                                                      in1=VV[:, k, :], op0=ALU.mult, op1=ALU.add)
                link(last)
            for q in range(4):
                ps = filled(dve, "cb", q)
                free(v.tensor_tensor(BV[:, 2 * q:2 * q + 2, :], two(ps), VV[:, 2 * q:2 * q + 2, :], ALU.mult), "cb", q)
            dve.wait_ge(*tiles["cb", 3][2])
            v.memset(ST[:, 31:32], 0.0).then_inc(sem("bv_done"), 8)
            residual("cout", (HT, modcol(MOD1 + 40)))
            norm(10)
            ff_pass("ff11")
            residual("acc_11", (HT, half_gate(MOD1 + 64, 0)))
            norm(11)


def _page_k(w):
    k, n = w.shape
    return w.reshape(k // P, P, n // FU, FU).transpose(2, 1, 0, 3).reshape(n // FU, P, PAGE)


def _ff_pages(g, u, d):
    n = g.shape[1] // FU
    gu = np.stack([g.reshape(KD, P, n, 2, P), u.reshape(KD, P, n, 2, P)], axis=4)
    gu = gu.transpose(2, 3, 1, 0, 4, 5).reshape(n, 2, P, PAGE)
    dn = d.reshape(n, 2, P, D).transpose(0, 2, 1, 3).reshape(n, 1, P, PAGE)
    return np.concatenate([gu, dn], axis=1)


def _cols(x):
    return np.ascontiguousarray(x, dtype=np.float32).reshape(-1, P).T


def kernel(**inputs):
    import concourse.bacc as _bacc
    from concourse.bass_utils import run_bass_kernel_spmd as _run

    a = {k: np.asarray(v) for k, v in inputs.items()}
    pg = np.zeros((NPAGES, P, PAGE), np.float32)

    def put(name, x, at=0, width=PAGE):
        p = PAGE_AT[name] + at
        pg[p:p + len(x), :, 0:width] = x

    ada, fin, mod = _page_k(a["w_ada"][0]), _page_k(a["w_ada_final"]), [_page_k(a["mod_w_2"][i]) for i in range(2)]
    w_in = a["w_in"][0]
    put("ada_a", ada[0:8])
    put("ada_b", ada[8:24])
    put("ada_f", fin)
    put("win_q", _page_k(w_in[:, 0:256]))
    put("win_kv", _page_k(w_in[:, 256:512]))
    put("win_f", _page_k(w_in[:, 544:1056]))
    put("win_g", _page_k(w_in[:, 1056:]))
    for name, key in (("uq", "w_uq"), ("uk", "w_uk"), ("uv", "w_uv")):
        w = a[key][0].reshape(KL, P, -1).transpose(1, 0, 2).reshape(1, P, -1)
        put(name, w, width=w.shape[2])
    for i, key in enumerate(("w_branch_attn", "w_branch_fourier")):
        w = a[key][0].reshape(4, P, 2, 512).transpose(2, 1, 0, 3).reshape(2, P, PAGE)
        put("br", w, at=2 * i)
    put("wout", _page_k(a["w_out"][0]))

    def ff(name, units, mods):
        p, n = PAGE_AT[name], len(units)
        turn = pg[p:p + 4 * n].reshape(n, 4, P, PAGE)
        turn[:, 0:2], turn[:, 3] = units[:, 0:2], units[:, 2]
        if mods is not None:
            turn[:, 2] = mods

    moe = np.concatenate([_ff_pages(a["w_expert_gate"][0, e], a["w_expert_up"][0, e], a["w_expert_down"][0, e])
                          for e in range(NEXP)])
    ffw = [[_ff_pages(a["ffn_w_gate_2"][i, j], a["ffn_w_up_2"][i, j], a["ffn_w_down_2"][i, j])
            for j in range(2)] for i in range(2)]
    ff("moe", moe, mod[0][0:32])
    put("m0_tail", mod[0][32:36])
    ff("ctx_ff", ffw[0][0], mod[1][0:11])
    ff("ff00", ffw[0][0], mod[1][11:22])
    put("m1_tail", mod[1][22:25])
    ff("ff01", ffw[0][1], mod[1][25:36])
    ff("ff10", ffw[1][0], None)
    ff("ff11", ffw[1][1], None)
    put("proj", _page_k(a["attn_w_in_2"][0]))
    put("aout", _page_k(a["attn_w_out_2"][0]))
    bg, cg, hh = (_page_k(a["conv_w_in_2"][0][:, i * D:(i + 1) * D]) for i in range(3))
    put("cin", np.concatenate([np.stack([cg, hh], 1).reshape(8, P, PAGE), bg]))
    put("cout", _page_k(a["conv_w_out_2"][0]))

    def tokens(x):
        return x.reshape(S, KD, P).transpose(2, 1, 0)

    acts = np.stack([tokens(a["x"]), tokens(a["ctx_2"])])
    vecs = np.concatenate([_cols(a[k]) for k in ("g_norm_mix", "g_norm_ffn", "g_norm_final", "norm_g_2", "final_g_2",
                                                 "b_gates", "conv_w_2", "g_q_lat", "g_kv_lat", "c", "c_2", "c_ctx_2",
                                                 "diff_subln_g_2")], axis=1)
    mb = np.concatenate([_cols(a["b_ada"]), _cols(a["b_ada_final"]), _cols(a["mod_b_2"])], axis=1)
    mb = np.stack([mb, mb], axis=2)

    f32 = np.float32
    rota = np.zeros((QKD, QKD), f32)
    for i in range(ROPE // 2):
        rota[NOPE + ROPE // 2 + i, NOPE + i] = -1.0
        rota[NOPE + i, NOPE + ROPE // 2 + i] = 1.0
    rotb = np.zeros((P, P), f32)
    for i in range(0, P, 2):
        rotb[i + 1, i] = -1.0
        rotb[i, i + 1] = 1.0
    invf = np.zeros((QKD, 1), f32)
    inv = np.power(f32(10000.0), -np.arange(0, ROPE, 2, dtype=f32) / f32(ROPE)).astype(f32)
    invf[NOPE:, 0] = np.concatenate([inv, inv])
    t = np.arange(S)
    inv2 = np.power(f32(10000.0), -np.arange(16, dtype=f32) / f32(16)).astype(f32)
    ang = np.concatenate([(t // GRID).astype(f32)[:, None] * inv2, (t % GRID).astype(f32)[:, None] * inv2], axis=1)
    ang = np.tile(np.repeat(ang, 2, axis=1), (1, 2)).T.astype(np.float64)
    csb = np.stack([np.cos(ang), np.sin(ang)], axis=1).astype(f32)
    th = 2 * np.pi * np.outer(np.arange(64), np.arange(64)) / 64
    dftd = np.zeros((P, 2, P), f32)
    for g in range(2):
        dftd[64 * g:64 * g + 64, 0, 64 * g:64 * g + 64] = np.cos(th)
        dftd[64 * g:64 * g + 64, 1, 64 * g:64 * g + 64] = np.sin(th)
    th = 2 * np.pi * (np.outer(t, t) % S) / S
    norm = 1.0 / np.sqrt(S * 64.0)
    dfts = (np.stack([np.cos(th), -np.sin(th)], axis=1) * norm).astype(f32)
    dfts = dfts.reshape(TB, P, 2, S).transpose(1, 0, 2, 3)
    rpb = a["na_rpb_2"][0]
    pad = np.zeros((NA_H, 15, 48 + 31 + 48), f32)
    pad[:, :, 48:79] = rpb
    bt = np.zeros((P, NA_H, 6, GRID), f32)
    for qc in range(GRID):
        strip = pad[:, :, 63 - qc:127 - qc]
        bt[qc] = strip[:, 5:11]
        bt[GRID + qc] = strip[:, 4:10]
    qc = np.arange(GRID)
    cs = np.clip(qc - 8, 0, GRID - 16)
    ok = (qc[None, :] >= cs[:, None]) & (qc[None, :] < cs[:, None] + 16)
    mask = np.tile(np.where(ok, f32(0), f32(NEG)), (2, 1)).astype(f32)
    wkr = w_in[:, 512:544].reshape(KD, P, ROPE).transpose(1, 0, 2)
    wrt = np.concatenate([a["w_router_group"][0], a["w_router_expert"][0].reshape(D, NEXP)], axis=1)
    wrt = wrt.reshape(KD, P, NG + NEXP).transpose(1, 0, 2)
    brt = np.concatenate([a["b_router_group"].reshape(-1), a["b_router_expert"].reshape(-1)])

    smalls = {"wkr": wkr, "rota": rota, "invf": invf, "pos": a["positions"].reshape(-1), "dftd": dftd, "dfts": dfts,
              "ident": np.eye(P, dtype=f32), "wrt": wrt, "brt": brt, "rev": np.arange(8, 0, -1).astype(f32),
              "rotb": rotb, "csb": csb, "bt": bt, "mask": mask, "lam": a["diff_lambda_2"][0].reshape(4, HD)}
    arrays = {"pages": pg, "acts": acts, "vecs": vecs, "mbias": mb, **smalls}
    arrays = {k: np.ascontiguousarray(v) for k, v in arrays.items()}
    nc = _bacc.Bacc("TRN2", target_bir_lowering=False, num_devices=1)
    ap = {k: nc.dram_tensor(f"in_{k}", v.shape, mybir.dt.from_np(v.dtype), kind="ExternalInput").ap()
          for k, v in arrays.items()}
    out = nc.dram_tensor("out_0", (P, KD, S), mybir.dt.float32, kind="ExternalOutput").ap()
    build(nc, ap["pages"], ap["acts"], ap["vecs"], ap["mbias"], {**{k: ap[k] for k in smalls}, "out": out})
    r = _run(nc, [{f"in_{k}": v for k, v in arrays.items()}], core_ids=[0])
    y = r.results[0]["out_0"]
    return y.transpose(2, 1, 0).reshape(1, S, D)
```

```python
import concourse.bass as bass
from concourse import mybir
from contextlib import ExitStack
import numpy as np

P = 128
D = 1024
KD = D // P
S = 256
TB = S // P
EPS = 1e-6
H1, NOPE, ROPE, VD = 8, 64, 32, 64
QKD = NOPE + ROPE
LORA = 256
KL = LORA // P
NG, NE8 = 4, 8
NEXP = NG * NE8
FU = 256
D_FF = 2816
FF_UNITS = D_FF // FU
NA_H, DF_H, HD = 8, 4, 64
NKT = 2 * TB
GRID = 64
LAM_INIT = 0.2
NEG = -1e30
PAGE = 2048
SLOTS = 3
UNIT_PAGES = 3
MSLOTS = 2

ADA, FIN, MOD0, MOD1 = 0, 48, 64, 136
NMOD = 208
_o = 0
VCOL = {}
for _n, _w in (("g_mix", 8), ("g_ffn", 8), ("g_fin1", 8), ("norm_g", 48), ("g_fin2", 8), ("b_gates", 16),
               ("conv_w", 24), ("g_q", 2), ("g_kv", 2), ("c", 24), ("subln", 1)):
    VCOL[_n] = _o
    _o += _w
NVEC = _o

PAGE_AT, _n = {}, 0
for _name, _c in (("win_q", 1), ("win_kv", 1), ("win_f", 2), ("win_g", 8), ("uq", 1), ("uk", 1),
                  ("uv", 1), ("br", 4), ("wout", 4), ("moe", NEXP * UNIT_PAGES), ("ctx_ff", FF_UNITS * UNIT_PAGES),
                  ("ff00", FF_UNITS * UNIT_PAGES), ("proj_a", 6), ("proj_b", 6), ("aout", 4),
                  ("ff01", FF_UNITS * UNIT_PAGES), ("ff10", FF_UNITS * UNIT_PAGES), ("cin", 12), ("cout", 4),
                  ("ff11", FF_UNITS * UNIT_PAGES)):
    PAGE_AT[_name] = _n
    _n += _c
NPAGES = _n

MOD_AT, _n = {}, 0
for _name, _c in (("first", 8), ("gates", 13), ("moe", NEXP), ("ctx_ff", FF_UNITS), ("ff00", FF_UNITS),
                  ("mixer", 1), ("ff01", FF_UNITS), ("ff10", FF_UNITS), ("cin", 6)):
    MOD_AT[_name] = _n
    _n += _c
NMODP = _n
assert 2 * NMODP == NMOD
MOE_ADA = (FIN + 16) // 2 - MOD_AT["moe"]
MOE_CTX = MOE_ADA + 10
assert 2 * (MOD_AT["moe"] + MOE_CTX - 1) >= MOD0 + 16


def build(nc, pages, mpages, acts, vecs, mbias, small):
    f32, f32r, bf16, i32 = mybir.dt.float32, mybir.dt.float32r, mybir.dt.bfloat16, mybir.dt.int32
    ALU, ACT, AX = mybir.AluOpType, mybir.ActivationFunctionType, mybir.AxisListType

    ctx = ExitStack()
    with ctx:
        def sb(name, shape, dt=f32):
            return ctx.enter_context(nc.sbuf_tensor(name, shape, dt))

        sems = {}

        def sem(name):
            if name not in sems:
                sems[name] = ctx.enter_context(nc.semaphore(name))
            return sems[name]

        raw = sb("raw", [P, SLOTS, PAGE])
        WH = sb("WH", [P, SLOTS, PAGE], f32r)
        WL = sb("WL", [P, SLOTS, PAGE], f32r)
        mraw = sb("mraw", [P, MSLOTS, PAGE])
        MACC = sb("MACC", [P, 2, 2, FU])
        HT = sb("HT", [P, KD, S])
        CT = sb("CT", [P, KD, S])
        YH = sb("YH", [P, KD, S], f32r)
        YL = sb("YL", [P, KD, S], f32r)
        YCH = sb("YCH", [P, KD, S], f32r)
        YCL = sb("YCL", [P, KD, S], f32r)
        XR = sb("XR", [P, KD, S])
        RT = sb("RT", [P, 2 * S])
        NA_ = sb("NA_", [P, KD])
        HG = sb("HG", [P, KD])
        MODT = sb("MODT", [P, NMOD, 2])
        MB = sb("MB", [P, NMOD, 2])
        V = sb("V", [P, NVEC])
        CA = sb("CA", [P, KD, 3])
        EPSC = sb("EPSC", [P, 1])
        ONES = sb("ONES", [P, P])
        ZW = sb("ZW", [P, P], bf16)
        SIL = sb("SIL", [P, 2, S])
        HH = sb("HH", [P, 2, S], f32r)
        HL = sb("HL", [P, 2, S], f32r)
        IDENT = sb("IDENT", [P, P])
        ROTB = sb("ROTB", [P, P])
        WRT = sb("WRT", [P, KD, NG + NEXP])
        BRT = sb("BRT", [P, NG + NEXP])
        REV = sb("REV", [P, NE8])
        INVF = sb("INVF", [QKD, 1])
        CTf = CT[:].rearrange("p k t -> p (k t)")
        DFTS = CTf[:, 0:1024].rearrange("p (t c n) -> p t c n", t=TB, c=2)
        DFTD = CTf[:, 1024:1280].rearrange("p (c n) -> p c n", c=2)
        WKR = CTf[:, 1280:1536].rearrange("p (k n) -> p k n", k=KD)
        ROTA = CTf[0:QKD, 1536:1536 + QKD]
        BTN = 5
        BT0 = CTf[:, 0:BTN * 6 * GRID].rearrange("p (h r c) -> p h r c", h=BTN, r=6)
        MASK = sb("MASK", [P, GRID])
        LAMT = sb("LAMT", [P, 8])
        ST = sb("ST", [P, 32])
        R = sb("R", [P, 11008])

        def reg(off, *dims, parts=P):
            n = int(np.prod(dims))
            v = R[0:parts, off:off + n]
            names = "abcd"[:len(dims)]
            if len(dims) == 1:
                return v
            return v.rearrange(f"p ({' '.join(names)}) -> p {' '.join(names)}",
                               **{names[i]: dims[i] for i in range(1, len(dims))})

        G = reg(0, 16, S)
        QK = reg(4096, 9, S, parts=QKD)
        POSI = reg(4096, S, parts=QKD).bitcast(i32)
        ANG = reg(4352, 2, S, parts=QKD)
        AK = reg(4864, 2, S, parts=QKD)
        U2 = reg(4096, TB, 2, 512)
        KH = reg(6400, H1, S, parts=QKD)
        QL = reg(6400, 4, S)
        V1 = reg(8448, TB, H1 * VD)
        FT = reg(9472, 4, S)
        LAMV = reg(9472, 4, HD)
        CSA = reg(10496, 2, S, parts=QKD)
        P1 = XR[:, 0:4, :].rearrange("p (a b) t -> p a b t", a=2)
        PT1 = XR[:, 4:8, :].rearrange("p (a b) t -> p a b t", a=2)
        RW = reg(4096, 8, 80)
        COMBT = reg(4096 + 640, S, parts=NEXP)
        CMASK = reg(4096 + 896, S, parts=NEXP)
        QA = reg(0, 4, S)
        KA = reg(1024, 4, 2 * S)
        VA = reg(3072, NKT, 512)
        P2 = reg(5120, 2, 2, 512)
        PT2 = reg(7168, 2, NKT, S)
        BT1 = reg(9216, NA_H - BTN, 6, GRID)
        CSB = reg(10368, 2, S)
        MG = XR[:, 4:8, :]
        CG = reg(0, KD, S)
        UU = reg(2048, KD, S + 2)
        VV = reg(4112, KD, S)
        BV = reg(6160, KD, S)

        def bias_of(h):
            return BT0[:, h, :, :] if h < BTN else BT1[:, h - BTN, :, :]

        PS = [ctx.enter_context(nc.psum_tensor(f"bank{b}", [P, 512], f32)) for b in range(8)]
        ACC, GU, MODB, MISC = (0, 1, 2, 3), (4, 5), 6, 7

        slot = [sem(f"page_in_{i}") for i in range(SLOTS)]
        mslot = [sem(f"mod_page_in_{i}") for i in range(MSLOTS)]
        s_hi = sem("page_hi")
        s_lo = sem("page_lo")
        s_page = sem("page_used")
        s_macc = sem("mod_summed")
        s_modp = sem("mod_product")
        s_tile = sem("tile_done")
        s_fa = sem("act_read_tile")
        s_fd = sem("dve_read_tile")
        s_modev = sem("mod_taken")
        s_hid = sem("hid_done")
        s_hx = sem("hid_step")
        s_mx = sem("mod_step")
        s_silu = sem("silu_done")
        s_sq = sem("norm_squares")
        s_rt, s_ri, s_xr, s_yf, s_y = (sem("norm_root"), sem("norm_coef"), sem("norm_scaled"), sem("norm_result"),
                                         sem("norm_split"))
        s_ac, s_dc = sem("act_chain"), sem("dve_chain")

        tiles, order = {}, []
        freed = {"act": 0, "dve": 0}
        done = [0]

        def tile(name, n, banks, reader, page=None, own=None, free=None):
            for i in range(n):
                ends = page(i) if callable(page) else None if page is None else page + i
                if own is not None:
                    ready = own
                elif ends is None:
                    done[0] += 1
                    ready = (s_tile, done[0])
                else:
                    ready = (s_page, ends + 1)
                if free is not None:
                    rel = free(i)
                else:
                    freed[reader] += 1
                    rel = ({"act": s_fa, "dve": s_fd}[reader], freed[reader])
                b = banks[i % len(banks)]
                tiles[name, i] = (b, ready, rel)
                order.append((name, i))

        PA = PAGE_AT

        def sums(name, page):
            tile(name, 4, ACC, "dve", page=lambda i: page if i == 3 else None)

        tile("ss0", 1, (MISC,), "act")
        tile("q", 1, (0,), "act", PA["win_q"])
        tile("kv", 1, (1,), "act", PA["win_kv"])
        tile("kr", 1, (2,), "act")
        tile("f", 2, (3, 4), "dve", PA["win_f"])
        tile("sslat", 1, (MISC,), "act")
        tile("g", 8, (0, 1, 2, 3), "act", PA["win_g"])
        for h in range(4):
            tile(f"qh{h}", 1, ((4, 5)[h % 2],), "act", page=PA["uq"] if h == 3 else None)
        for h in range(2):
            tile(f"kh{h}", 1, ((4, 5)[h % 2],), "dve", page=PA["uk"] if h == 1 else None)
        tile("v0", 1, (0,), "dve")
        tile("v1", 1, (1,), "dve", PA["uv"])
        tile("rot", 5, (2, 3, 4, 5, 7), "dve")
        for h in range(H1):
            tile(f"s{h}", 1, ((0, 1)[h % 2],), None, free=lambda i, h=h: (sem("exp1"), h + 1))
            if h >= 1:
                tile(f"pt{h - 1}", 1, (2,), None, free=lambda i, h=h: (sem("pt1"), h))
                if (h - 1) % 2 == 0:
                    tile(f"o{(h - 1) // 2}", 1, ((3, 7)[((h - 1) // 2) % 2],), "dve",
                         own=(sem("o1_done"), (h - 1) // 2 + 1))
        tile("pt7", 1, (2,), None, free=lambda i: (sem("pt1"), 8))
        tile("fd", 4, (4, 5), "dve")
        tile("fs", 2, (0, 1), "dve")
        tile("bra", 4, (2, 3), "dve", page=lambda i: PA["br"] + i // 2)
        tile("brf", 4, (4, 5), "dve", page=lambda i: PA["br"] + 2 + i // 2)
        tile("wout", 4, (0, 1), "dve", PA["wout"])
        tile("ss1", 1, (MISC,), "act")
        tile("rt", 1, (0,), "dve")
        tile("ct", 1, (1,), "dve")
        tile("ss2", 1, (MISC,), "act")
        sums("acc_moe", PA["moe"] + NEXP * UNIT_PAGES - 1)
        tile("ss3", 1, (MISC,), "act")
        tile("ss4", 1, (MISC,), "act")
        sums("acc_ctx", PA["ctx_ff"] + FF_UNITS * UNIT_PAGES - 1)
        tile("ss5", 1, (MISC,), "act")
        sums("acc_00", PA["ff00"] + FF_UNITS * UNIT_PAGES - 1)
        tile("kac0", 1, (4,), "act")
        tile("ss6", 1, (MISC,), "act")
        tile("kac1", 1, (5,), "act")
        tile("kax", 2, (0, 1), "act", page=PA["proj_a"])
        for i in range(2):
            tile(f"va{i}", 2, ((2, 3), (4, 5))[i], "dve", page=lambda j, i=i: PA["proj_a"] + 2 + i)
        tile("qa", 2, (0, 1), "act", PA["proj_a"] + 4)
        NA_N = NA_H * TB
        for a in range(NA_N + 1):
            if a < NA_N:
                tile(f"sa{a}", 1, ((0, 1)[a % 2],), None, free=lambda i, a=a: (sem("exp2"), a + 1))
            if a >= 1:
                tile(f"pta{a - 1}", 1, ((2, 3)[(a - 1) % 2],), None, free=lambda i, a=a: (sem("pt2"), a))
                if (a - 1) % 4 == 1:
                    tile(f"oa{(a - 1) // 4}", 1, ((4, 5)[((a - 1) // 4) % 2],), "dve",
                         own=(sem("oa_done"), (a - 1) // 4 + 1))
        tile("qb", 2, (0, 1), "act", PA["proj_b"])
        for i in range(2):
            tile(f"kb{i}", 2, ((2, 3), (0, 1))[i], "act", page=lambda j, i=i: PA["proj_b"] + 2 + i)
        for i in range(2):
            tile(f"vb{i}", 2, ((4, 5), (0, 1))[i], "dve", page=lambda j, i=i: PA["proj_b"] + 4 + i)
        tile("rotb", 4, (2, 3, 4, 5), "dve")
        DF_N = DF_H * TB
        for a in range(DF_N + 1):
            if a < DF_N:
                for m in range(2):
                    tile(f"sd{2 * a + m}", 1, ((0, 1, 4, 5)[(2 * a + m) % 4],), None,
                         free=lambda i, a=a, m=m: (sem("exp3"), 2 * a + m + 1))
            if a >= 1:
                tile(f"ptd{a - 1}", 1, ((2, 3)[(a - 1) % 2],), None, free=lambda i, a=a: (sem("pt3"), a))
                if (a - 1) % 2 == 1:
                    tile(f"od{(a - 1) // 2}", 1, (MISC,), "dve")
        tile("sssub", 2, (0, 1), "act")
        tile("aout", 4, (2, 3), "dve", PA["aout"])
        tile("ss7", 1, (MISC,), "act")
        sums("acc_01", PA["ff01"] + FF_UNITS * UNIT_PAGES - 1)
        tile("ss8", 1, (MISC,), "act")
        sums("acc_10", PA["ff10"] + FF_UNITS * UNIT_PAGES - 1)
        tile("ss9", 1, (MISC,), "act")
        for i in range(4):
            tile(f"cg{i}", 1, ((0, 1)[i % 2],), "act", page=lambda j, i=i: PA["cin"] + 2 * i)
            tile(f"ch{i}", 1, ((2, 3)[i % 2],), "dve", page=lambda j, i=i: PA["cin"] + 2 * i + 1)
        tile("cb", 4, (4, 5), "dve", PA["cin"] + 8)
        tile("cout", 4, (0, 1), "dve", PA["cout"])
        tile("ss10", 1, (MISC,), "act")
        sums("acc_11", PA["ff11"] + FF_UNITS * UNIT_PAGES - 1)
        tile("ss11", 1, (MISC,), "act")

        prev_free, last = {}, {}
        for key in order:
            b, _, rel = tiles[key]
            prev_free[key] = last.get(b)
            last[b] = rel

        def bank(name, i=0):
            return PS[tiles[name, i][0]]

        def opened(pe, name, i=0):
            if prev_free[name, i] is not None:
                pe.wait_ge(*prev_free[name, i])
            return bank(name, i)

        def filled(eng, name, i=0):
            eng.wait_ge(*tiles[name, i][1])
            return bank(name, i)

        OPERANDS = {"y": (YH, YL), "yc": (YCH, YCL)}
        NORMS = [
            (HT, "y", "g_mix", 0, ADA + 8, ADA, 0),
            (HT, "y", "g_ffn", 0, ADA + 32, ADA + 24, 0),
            (CT, "yc", "norm_g", 0, MOD0 + 8, MOD0, 1),
            (HT, "h", "g_fin1", 0, FIN + 8, FIN, 0),
            (HT, "y", "norm_g", 0, MOD0 + 8, MOD0, 0),
            (CT, "yc", "norm_g", 8, MOD0 + 32, MOD0 + 24, 1),
            (HT, "y", "norm_g", 8, MOD0 + 32, MOD0 + 24, 0),
            (HT, "y", "norm_g", 16, MOD0 + 56, MOD0 + 48, 0),
            (HT, "y", "norm_g", 24, MOD1 + 8, MOD1, 0),
            (HT, "y", "norm_g", 32, MOD1 + 32, MOD1 + 24, 0),
            (HT, "y", "norm_g", 40, MOD1 + 56, MOD1 + 48, 0),
            (HT, None, "g_fin2", 0, None, None, 0),
        ]
        NCH = 4
        SPLITS = [sum(1 for x in NORMS[:n] if x[1] in OPERANDS) for n in range(len(NORMS) + 1)]
        N_SMALL, N_MID = 12, 4

        PASSES, _u = {}, 0
        for name, n, src, routed, acc, parts in (
                ("moe", NEXP, "y", True, "acc_moe", ((MOE_ADA, (0,)), (MOE_CTX - MOE_ADA, (1, 2)), (NEXP - MOE_CTX, (1, 2)))),
                ("ctx_ff", FF_UNITS, "yc", False, "acc_ctx", ((2, (1,)), (FF_UNITS - 2, (1,)))),
                ("ff00", FF_UNITS, "y", False, "acc_00", ((2, (1,)), (FF_UNITS - 2, (1,)))),
                ("ff01", FF_UNITS, "y", False, "acc_01", ((FF_UNITS, (1,)),)),
                ("ff10", FF_UNITS, "y", False, "acc_10", ((FF_UNITS, (1,)),)),
                ("ff11", FF_UNITS, "y", False, "acc_11", ((FF_UNITS, ()),))):
            PASSES[name] = (PA[name], _u, n, src, routed, acc, parts)
            _u += n

        def units(eng, parts, unit, between=()):
            u = 0
            for j, (n, vectors) in enumerate(parts):
                if n == 2:
                    unit(u, 0, vectors)
                    unit(u + 1, 0, vectors)
                else:
                    with eng.Fori(0, n // 2) as i:
                        unit(u, i, vectors)
                        unit(u + 1, i, vectors)
                if n % 2:
                    unit(u + n - 1, 0, vectors)
                if j < len(between):
                    between[j]()
                u += n

        block = ctx.enter_context(nc.Block())

        @block.sync
        def _(sp):
            def page(p, i=0):
                if p >= SLOTS:
                    sp.wait_ge(s_lo, i * 2 * UNIT_PAGES + (p + 1 - SLOTS))
                sp.dma_start(raw[:, p % SLOTS, :], pages[i * 2 * UNIT_PAGES + p]).then_inc(slot[p % SLOTS], 16)

            def mod_page(m, i=0):
                if m >= MSLOTS:
                    sp.wait_ge(s_macc, i * 2 + (m + 1 - MSLOTS))
                sp.dma_start(mraw[:, m % MSLOTS, :], mpages[i * 2 + m]).then_inc(mslot[m % MSLOTS], 16)

            for m in range(MOD_AT["gates"]):
                mod_page(m)
                if m == MOD_AT["gates"] - 3:
                    page(0)
            for p in range(1, SLOTS):
                page(p)
            for p in range(SLOTS, PA["win_g"]):
                page(p)
            m = MOD_AT["gates"]
            for p in range(PA["win_g"], PA["moe"]):
                page(p)
                if m < MOD_AT["moe"]:
                    mod_page(m)
                    m += 1
            for name in ("moe", "ctx_ff", "ff00", "mixer", "ff01", "ff10", "cin", "ff11"):
                if name == "mixer":
                    for p in range(PA["proj_a"], PA["ff01"]):
                        page(p)
                    mod_page(MOD_AT["mixer"])
                elif name == "cin":
                    for p in range(PA["cin"], PA["ff11"]):
                        page(p)
                        m = p - PA["cin"]
                        if m % 2 == 0 and m // 2 < NMODP - MOD_AT["cin"]:
                            mod_page(MOD_AT["cin"] + m // 2)
                else:
                    def unit(u, i, vectors, name=name):
                        for q in range(UNIT_PAGES):
                            page(PA[name] + UNIT_PAGES * u + q, i)
                        if vectors:
                            mod_page(MOD_AT[name] + u, i)

                    units(sp, PASSES[name][6], unit)

        @block.gpsimd
        def _(pool):
            def rest(p, i=0):
                pool.wait_ge(s_hi, i * SLOTS + (p + 1))
                nc.gpsimd.tensor_tensor(WL[:, p % SLOTS, :], raw[:, p % SLOTS, :], WH[:, p % SLOTS, :].bitcast(f32),
                                        ALU.subtract).then_inc(s_lo, 1)

            with pool.Fori(0, NPAGES // SLOTS) as i:
                for q in range(SLOTS):
                    rest(q, i)
            for p in range(NPAGES // SLOTS * SLOTS, NPAGES):
                rest(p)

        @block.tensor
        def _(pe):
            mm = nc.tensor.matmul

            def mm3(out, w, x, start, stop):
                mm(out, w[0], x[0], start=start, stop=False, skip_group_check=True)
                mm(out, w[0], x[1], start=False, stop=False, skip_group_check=True)
                return mm(out, w[1], x[0], start=False, stop=stop, skip_group_check=True)

            def mm3x(out, x, w, start, stop):
                mm(out, x[0], w[0], start=start, stop=False, skip_group_check=True)
                mm(out, x[1], w[0], start=False, stop=False, skip_group_check=True)
                return mm(out, x[0], w[1], start=False, stop=stop, skip_group_check=True)

            def arrived(p, i=0):
                pe.wait_ge(s_lo, i * 2 * UNIT_PAGES + (p + 1))
                return WH[:, p % SLOTS, :], WL[:, p % SLOTS, :]

            def shaped(pair, pattern, **sizes):
                return [x.rearrange(pattern, **sizes) for x in pair]

            def mod_product(m, i=0, nv=1):
                pe.wait_ge(s_macc, i * 2 + (m + 1))
                if m:
                    pe.wait_ge(s_modev, i * 2 + m)
                for b in range(2):
                    for vi in range(nv):
                        last = mm(PS[MODB][:, 2 * b + vi:2 * b + vi + 1], MACC[:, m % 2, vi, b * P:(b + 1) * P],
                                  ONES[:, 0:1], start=True, stop=True, skip_group_check=True)
                last.then_inc(s_modp, 1)

            def norm(n):
                ps = opened(pe, f"ss{n}")
                for k in range(KD):
                    if k % 2 == 0:
                        pe.wait_ge(s_sq, NCH * n + k // 2 + 1)
                    last = mm(ps[:, 0:S], ONES[:], XR[:, k, :], start=(k == 0), stop=(k == KD - 1))
                last.then_inc(s_tile, 1)

            def y_ready(n, k=KD - 1):
                pe.wait_ge(s_y, NCH * SPLITS[n] + k // 2 + 1)

            def linear(p, ps, x, ready=None, k_tiles=KD, wcol=FU, off=0, inc=True):
                w = shaped([a[:, 0:k_tiles * wcol] for a in arrived(p)], "p (k n) -> p k n", k=k_tiles)
                for b in range(2):
                    c = off + b * P
                    for k in range(k_tiles):
                        if ready is not None and b == 0 and k % 2 == 0:
                            ready(k)
                        last = mm3(ps[:, b * S:(b + 1) * S], [a[:, k, c:c + P] for a in w], [a[:, k, :] for a in x],
                                   k == 0, k == k_tiles - 1)
                if inc:
                    last.then_inc(s_page, 1)
                return last

            Y, YC = (YH, YL), (YCH, YCL)

            def ff_pass(name, norm_of, between=()):
                p0, u0, n, src, routed, acc, parts = PASSES[name]
                x = OPERANDS[src]
                before(acc)
                for b in range(4):
                    ps = opened(pe, acc, b)
                    mm(ps[:, :], ZW[:], ZW[:, 0:1].broadcast_to([P, 512]), start=True, stop=True, skip_group_check=True)
                for b in (*GU, MISC) if routed else GU:
                    rel = last_read[b]
                    if rel is not None:
                        pe.wait_ge(*rel)

                def unit(u, i, vectors):
                    p, U = p0 + UNIT_PAGES * u, u0 + u
                    if routed:
                        pe.wait_ge(sem("cmask"), i * 2 + (u + 1))
                        mm(PS[MISC][:, 0:S], ONES[0:NEXP, :], CMASK, start=True, stop=True, skip_group_check=True)
                    for j in range(2):
                        w = shaped(arrived(p + j, i), "p (k g n) -> p k g n", k=KD, g=2)
                        pe.wait_ge(s_hid, i * 4 + (2 * U + j + 1))
                        for g in range(2):
                            for k in range(KD):
                                if u == 0 and j == 0 and g == 0 and k % 2 == 0:
                                    y_ready(norm_of, k)
                                last = mm3(PS[GU[j]][:, g * S:(g + 1) * S], [a[:, k, g, :] for a in w],
                                           [a[:, k, :] for a in x], k == 0, k == KD - 1)
                        last.then_inc(s_page, 1)
                    if vectors:
                        mod_product(MOD_AT[name] + u - 1, i, len(vectors))
                    w = shaped(arrived(p + 2, i), "p (j n) -> p j n", j=2)

                    def down(b, j):
                        return mm3(PS[ACC[b // 2]][:, (b % 2) * S:(b % 2 + 1) * S],
                                   [a[:, j, b * P:(b + 1) * P] for a in w], (HH[:, j, :], HL[:, j, :]), False, True)

                    if u == n - 1:
                        pe.wait_ge(s_hid, 2 * U + 4)
                        for b in range(KD):
                            for j in range(2):
                                last = down(b, j)
                            if b % 2 and b < KD - 1:
                                last.then_inc(s_tile, 1)
                    else:
                        for j in range(2):
                            pe.wait_ge(s_hid, i * 4 + (2 * U + j + 3))
                            for b in range(KD):
                                last = down(b, j)
                    last.then_inc(s_page, 1)

                units(pe, parts, unit, between)

            last_read = {}

            def before(name):
                last_read.clear()
                for b in range(8):
                    last_read[b] = None
                for key in order:
                    if key[0] == name:
                        break
                    if key[0] != "ss2":
                        last_read[tiles[key][0]] = tiles[key][2]

            pe.wait_ge(sem("ones"), 1)
            for m in range(MOD_AT["gates"]):
                mod_product(m)
            norm(0)
            linear(PA["win_q"], opened(pe, "q"), Y, ready=lambda k: y_ready(0, k))
            linear(PA["win_kv"], opened(pe, "kv"), Y)
            pe.wait_ge(sem("in_small"), 16 * N_SMALL)
            pe.wait_ge(s_yf, NCH)
            ps = opened(pe, "kr")
            for k in range(KD):
                last = mm(ps[NOPE:QKD, 0:S], WKR[:, k, :], XR[:, k, :], start=(k == 0), stop=(k == KD - 1))
            last.then_inc(s_tile, 1)
            for q in range(2):
                linear(PA["win_f"] + q, opened(pe, "f", q), Y)
            ps = opened(pe, "sslat")
            pe.wait_ge(sem("lat_sq"), 1)
            for t in range(2):
                for k in range(KL):
                    last = mm(ps[:, t * S:(t + 1) * S], ONES[:], XR[:, t * KL + k, :], start=(k == 0), stop=(k == KL - 1))
            last.then_inc(s_tile, 1)
            m = MOD_AT["gates"]
            for q in range(8):
                linear(PA["win_g"] + q, opened(pe, "g", q), Y)
                mod_product(m)
                m += 1
            pe.wait_ge(sem("lat_n"), 1)
            w = shaped([a[:, 0:KL * H1 * QKD] for a in arrived(PA["uq"])], "p (k h n) -> p k h n", k=KL, h=H1)
            for t in range(4):
                ps = opened(pe, f"qh{t}")
                for hh in range(2):
                    for k in range(KL):
                        last = mm3(ps[0:QKD, hh * S:(hh + 1) * S], [a[:, k, 2 * t + hh, :] for a in w],
                                   [a[:, k, :] for a in YC], k == 0, k == KL - 1)
                last.then_inc(s_tile if t < 3 else s_page, 1)
            mod_product(m)
            m += 1
            pe.wait_ge(sem("lat_n"), 2)
            w = shaped([a[:, 0:KL * H1 * NOPE] for a in arrived(PA["uk"])], "p (k h n) -> p k h n", k=KL, h=H1 // 2)
            for t in range(2):
                ps = opened(pe, f"kh{t}")
                for hh in range(2):
                    for k in range(KL):
                        last = mm3(ps[:, hh * S:(hh + 1) * S], [a[:, k, 2 * t + hh, :] for a in w],
                                   [a[:, KL + k, :] for a in YC], k == 0, k == KL - 1)
                last.then_inc(s_tile if t < 1 else s_page, 1)
            mod_product(m)
            m += 1
            w = shaped([a[:, 0:KL * H1 * VD] for a in arrived(PA["uv"])], "p (k n) -> p k n", k=KL)
            for t in range(TB):
                ps = opened(pe, f"v{t}")
                for k in range(KL):
                    last = mm3x(ps[:, :], [a[:, KL + k, t * P:(t + 1) * P] for a in YC], [a[:, k, :] for a in w],
                                k == 0, k == KL - 1)
                last.then_inc(s_tile if t < TB - 1 else s_page, 1)
            mod_product(m)
            m += 1
            pe.wait_ge(s_fa, tiles["qh3", 0][2][1])
            pe.wait_ge(sem("kr_zero"), 1)
            QKf = QK.rearrange("p h t -> p (h t)")
            for t in range(5):
                n = 512 if t < 4 else S
                ps = opened(pe, "rot", t)
                mm(ps[0:QKD, 0:n], ROTA[:], QKf[:, t * 512:t * 512 + n], start=True, stop=True).then_inc(s_tile, 1)
            mod_product(m)

            def scores1(h):
                ps = opened(pe, f"s{h}")
                if h == 0:
                    pe.wait_ge(sem("rope1"), 1)
                for qb in range(TB):
                    last = mm(ps[:, qb * S:(qb + 1) * S], QK[:, h, qb * P:(qb + 1) * P], KH[:, h, :],
                              start=True, stop=True)
                last.then_inc(s_tile, 1)

            def turn1(h):
                ps = opened(pe, f"pt{h}")
                pe.wait_ge(sem("pn1"), h + 1)
                for kb in range(TB):
                    for qb in range(TB):
                        last = nc.tensor.transpose(ps[:, kb * S + qb * P:kb * S + (qb + 1) * P],
                                                   P1[:, h % 2, qb, kb * P:(kb + 1) * P], IDENT[:])
                last.then_inc(s_tile, 1)

            def pv1(h):
                if h % 2 == 0:
                    opened(pe, f"o{h // 2}")
                ps = bank(f"o{h // 2}")
                pe.wait_ge(sem("pt1"), h + 1)
                o = VD * (h % 2)
                for kb in range(TB):
                    last = mm(ps[o:o + VD, 0:S], V1[:, kb, h * VD:(h + 1) * VD], PT1[:, h % 2, kb, :],
                              start=(kb == 0), stop=(kb == TB - 1), skip_group_check=True)
                return last

            for h in range(H1 + 1):
                if h < H1:
                    scores1(h)
                if h >= 1:
                    turn1(h - 1)
                    last = pv1(h - 1)
                    if (h - 1) % 2 == 1:
                        last.then_inc(sem("o1_done"), 1)
            pe.wait_ge(s_fd, tiles["f", 1][2][1])
            for t in range(4):
                tb, fp = t // 2, t % 2
                ps = opened(pe, "fd", t)
                for q in range(2):
                    last = mm(ps[:, q * S:(q + 1) * S], FT[:, 2 * fp + q, tb * P:(tb + 1) * P],
                              DFTD[:].rearrange("p c n -> p (c n)"), start=True, stop=True)
                last.then_inc(s_tile, 1)
            pe.wait_ge(s_fd, tiles["fd", 3][2][1])
            for t in range(2):
                ps = opened(pe, "fs", t)
                for q in range(2):
                    ft = 2 * t + q
                    for c in range(4):
                        last = mm(ps[:, q * S:(q + 1) * S], U2[:, c // 2, c % 2, ft * P:(ft + 1) * P],
                                  DFTS[:, c // 2, c % 2, :], start=(c == 0), stop=(c == 3))
                last.then_inc(s_tile, 1)
            for t, (nm, x) in enumerate((("bra", [a[:, 0:4, :] for a in Y]), ("brf", [a[:, 4:8, :] for a in Y]))):
                if t == 0:
                    pe.wait_ge(sem("at_done"), 4)
                else:
                    pe.wait_ge(sem("fo_done"), 2)
                for q in range(4):
                    ps = opened(pe, nm, q)
                    linear(PA["br"] + 2 * t + q // 2, ps, x, k_tiles=4, wcol=512, off=(q % 2) * S, inc=(q % 2 == 1))
            for q in range(4):
                ps = opened(pe, "wout", q)
                linear(PA["wout"] + q, ps, YC,
                       ready=(lambda k: pe.wait_ge(sem("merged"), k // 2 + 1)) if q == 0 else None)
            norm(1)
            pe.wait_ge(s_yf, 2 * NCH)
            ps = opened(pe, "rt")
            for t in range(TB):
                for k in range(KD):
                    last = mm(ps[:, t * 64:t * 64 + NG + NEXP], XR[:, k, t * P:(t + 1) * P], WRT[:, k, :],
                              start=(k == 0), stop=(k == KD - 1))
            last.then_inc(s_tile, 1)
            ps = opened(pe, "ct")
            pe.wait_ge(sem("comb"), 1)
            for t in range(TB):
                last = nc.tensor.transpose(ps[0:NEXP, t * P:(t + 1) * P], RW[:, 7, t * NEXP:(t + 1) * NEXP], IDENT[:])
            last.then_inc(s_tile, 1)

            def context_norm():
                norm(2)
                pe.wait_ge(*tiles["ss2", 0][2])

            ff_pass("moe", 1, (lambda: None, context_norm))
            norm(3)

            ff_pass("ctx_ff", 2, (lambda: norm(4),))
            ff_pass("ff00", 4, (lambda: norm(5),))
            mod_product(MOD_AT["mixer"] - 1)
            y_ready(5)
            linear(PA["proj_a"], opened(pe, "kac0"), YC, inc=False).then_inc(s_tile, 1)
            norm(6)
            linear(PA["proj_a"] + 1, opened(pe, "kac1"), YC, inc=False).then_inc(s_tile, 1)
            for q in range(2):
                linear(PA["proj_a"] + q, opened(pe, "kax", q), Y, ready=(lambda k: y_ready(6, k)) if q == 0 else None)

            def keys(nm, base):
                for q in range(2):
                    for c, x in ((0, Y), (1, YC)):
                        linear(base + q, opened(pe, f"{nm}{q}", c), x, inc=(c == 1))

            def values(nm, base):
                for q in range(2):
                    w = shaped(arrived(base + q), "p (k n) -> p k n", k=KD)
                    for c, x in ((0, Y), (1, YC)):
                        ps = opened(pe, f"{nm}{q}", c)
                        for t in range(TB):
                            for k in range(KD):
                                last = mm3x(ps[:, t * S:(t + 1) * S], [a[:, k, t * P:(t + 1) * P] for a in x],
                                            [a[:, k, :] for a in w], k == 0, k == KD - 1)
                    last.then_inc(s_page, 1)

            values("va", PA["proj_a"] + 2)
            for q in range(2):
                linear(PA["proj_a"] + 4 + q, opened(pe, "qa", q), Y)

            def turn2(name, semn, a, src):
                ps = opened(pe, name)
                pe.wait_ge(sem(semn), a + 1)
                for kt in range(NKT):
                    last = nc.tensor.transpose(ps[:, kt * P:(kt + 1) * P], src[:, kt * P:(kt + 1) * P], IDENT[:])
                last.then_inc(s_tile, 1)

            for a in range(NA_N + 1):
                if a < NA_N:
                    h, qb = a // TB, a % TB
                    o = HD * (h % 2)
                    if a == 0:
                        pe.wait_ge(s_fa, tiles["qa", 1][2][1])
                        pe.wait_ge(s_fd, tiles["va1", 1][2][1])
                    ps = opened(pe, f"sa{a}")
                    mm(ps[:, :], QA[o:o + HD, h // 2, qb * P:(qb + 1) * P], KA[o:o + HD, h // 2, :],
                       start=True, stop=True).then_inc(s_tile, 1)
                if a >= 1:
                    b = a - 1
                    h, qb = b // TB, b % TB
                    turn2(f"pta{b}", "pn2", b, P2[:, b % 2, 0, :])
                    if qb == 1:
                        if h % 2 == 0:
                            opened(pe, f"oa{h // 2}")
                        ps = bank(f"oa{h // 2}")
                        pe.wait_ge(sem("pt2"), b + 1)
                        o = HD * (h % 2)
                        for kt in range(NKT):
                            last = mm(ps[o:o + HD, 0:S], VA[:, kt, h * HD:(h + 1) * HD], PT2[:, h % 2, kt, :],
                                      start=(kt == 0), stop=(kt == NKT - 1), skip_group_check=True)
                        if h % 2 == 1:
                            last.then_inc(sem("oa_done"), 1)
            for q in range(2):
                linear(PA["proj_b"] + q, opened(pe, "qb", q), Y)
            keys("kb", PA["proj_b"] + 2)
            values("vb", PA["proj_b"] + 4)
            pe.wait_ge(s_fa, tiles["kb1", 1][2][1])
            pe.wait_ge(sem("in_mid"), 16 * N_MID)
            for t in range(4):
                ps = opened(pe, "rotb", t)
                for q in range(2):
                    x = QA[:, 2 * t + q, :] if t < 2 else KA[:, 2 * (t - 2) + q, 0:S]
                    last = mm(ps[:, q * S:(q + 1) * S], ROTB[:], x, start=True, stop=True)
                last.then_inc(s_tile, 1)
            for a in range(DF_N + 1):
                if a < DF_N:
                    h, qb = a // TB, a % TB
                    if a == 0:
                        pe.wait_ge(sem("rope2"), 1)
                    for mp in range(2):
                        o = HD * mp
                        ps = opened(pe, f"sd{2 * a + mp}")
                        mm(ps[:, :], QA[o:o + HD, h, qb * P:(qb + 1) * P], KA[o:o + HD, h, :],
                           start=True, stop=True).then_inc(s_tile, 1)
                if a >= 1:
                    b = a - 1
                    h, qb = b // TB, b % TB
                    turn2(f"ptd{b}", "pn3", b, P2[:, b % 2, 0, :])
                    if qb == 1:
                        ps = opened(pe, f"od{h}")
                        pe.wait_ge(sem("pt3"), b + 1)
                        for kt in range(NKT):
                            last = mm(ps[:, 0:S], VA[:, kt, h * P:(h + 1) * P], PT2[:, h % 2, kt, :],
                                      start=(kt == 0), stop=(kt == NKT - 1))
                        last.then_inc(s_tile, 1)
            for t in range(2):
                ps = opened(pe, "sssub", t)
                pe.wait_ge(sem("sub_sq"), t + 1)
                mm(ps[:, :], ONES[:], XR[:, 2 * t:2 * t + 2, :].rearrange("p a t -> p (a t)"),
                   start=True, stop=True).then_inc(s_tile, 1)
            for q in range(4):
                ps = opened(pe, "aout", q)
                if q == 0:
                    pe.wait_ge(sem("sub_norm"), 2)
                linear(PA["aout"] + q, ps, Y)
            norm(7)
            ff_pass("ff01", 7)
            norm(8)
            ff_pass("ff10", 8)
            norm(9)
            for q in range(4):
                linear(PA["cin"] + 2 * q, opened(pe, f"cg{q}"), Y, ready=lambda k: y_ready(9, k))
                linear(PA["cin"] + 2 * q + 1, opened(pe, f"ch{q}"), Y)
                mod_product(MOD_AT["cin"] - 1 + q)
            for q in range(4):
                linear(PA["cin"] + 8 + q, opened(pe, "cb", q), Y)
                if q < 3:
                    mod_product(MOD_AT["cin"] + 3 + q)
            for q in range(4):
                ps = opened(pe, "cout", q)
                linear(PA["cout"] + q, ps, YC,
                       ready=(lambda k: pe.wait_ge(sem("bv_done"), k // 2 + 1)) if q == 0 else None)
            norm(10)
            ff_pass("ff11", 10)
            norm(11)

        @block.scalar
        def _(act):
            f = nc.scalar.activation
            chain = [0]

            def link(ins):
                chain[0] += 1
                ins.then_inc(s_ac, 1)
                act.wait_ge(s_ac, chain[0])

            def free(ins, name, i=0):
                assert tiles[name, i][2][0] is s_fa or tiles[name, i][2][0] == s_fa
                ins.then_inc(s_fa, 1)

            def norm(n, src_ready=None):
                norm_squares(n, src_ready)
                norm_result(n)

            def norm_squares(n, src_ready=None):
                src = NORMS[n][0]
                if n:
                    act.wait_ge(s_yf, NCH * n)
                    act.wait_ge(s_y, NCH * SPLITS[n])
                for c in range(NCH):
                    if src_ready is not None:
                        src_ready(c)
                    f(XR[:, 2 * c:2 * c + 2, :], src[:, 2 * c:2 * c + 2, :], ACT.Square).then_inc(s_sq, 1)

            def norm_result(n):
                src, dst, _, _, sc, sh, vi = NORMS[n]
                ps = filled(act, f"ss{n}")
                free(f(RT[:, 0:S], ps[:, 0:S], ACT.Sqrt, bias=EPSC[:, 0:1], scale=1.0 / D), f"ss{n}")
                out = HT if dst == "h" else XR
                for c in range(NCH):
                    act.wait_ge(s_xr, NCH * n + c + 1)
                    for k in (2 * c, 2 * c + 1):
                        if sh is None:
                            last = f(out[:, k, :], XR[:, k, :], ACT.Copy, scale=NA_[:, k:k + 1])
                        else:
                            last = f(out[:, k, :], XR[:, k, :], ACT.Identity, scale=NA_[:, k:k + 1],
                                     bias=MODT[:, sh + k, vi:vi + 1])
                    last.then_inc(s_yf, 1)

            def split(p, i=0):
                if p >= SLOTS:
                    act.wait_ge(s_page, i * 2 * UNIT_PAGES + (p + 1 - SLOTS))
                act.wait_ge(slot[p % SLOTS], i * (2 * UNIT_PAGES // SLOTS * 16) + 16 * (p // SLOTS + 1))
                f(WH[:, p % SLOTS, :], raw[:, p % SLOTS, :], ACT.Copy).then_inc(s_hi, 1)

            at = [0]

            def after(p):
                while at[0] <= min(p + SLOTS, NPAGES - 1):
                    split(at[0])
                    at[0] += 1

            def ff_pass(name, between=()):
                p0, u0, n, src, routed, acc, parts = PASSES[name]
                assert at[0] == p0 + SLOTS

                def unit(u, i, vectors):
                    p = p0 + UNIT_PAGES * u
                    for j in range(2):
                        act.wait_ge(s_page, i * 2 * UNIT_PAGES + (p + j + 1))
                        f(SIL[:, j, :], PS[GU[j]][:, 0:S], ACT.Silu).then_inc(s_silu, 1)
                        if p + j + SLOTS < NPAGES:
                            split(p + j + SLOTS, i)
                    if p + 2 + SLOTS < NPAGES:
                        split(p + 2 + SLOTS, i)

                units(act, parts, unit, between)
                at[0] = p0 + UNIT_PAGES * n + SLOTS

            def soft_exp(out, ps, bias, total):
                return f(out, ps, ACT.Exp, bias=bias, accum_out=total)

            for dst, src, s_in in ((V[:], vecs, "in_vecs"), (HT[:], acts[0], "in_x"), (MB[:], mbias, "in_mb")):
                act.dma_start(dst, src).then_inc(sem(s_in), 16)
            act.wait_ge(sem("in_vecs"), 16)
            f(CA[:].rearrange("p k v -> p v k"), V[:, VCOL["c"]:VCOL["c"] + 24].rearrange("p (v k) -> p v k", v=3),
              ACT.Silu).then_inc(sem("silu_c"), 1)
            for dst, src, s_in in ((POSI, small["pos"].partition_broadcast(QKD), "in_small"),
                                   (INVF[:], small["invf"], "in_small"), (WKR, small["wkr"], "in_small"),
                                   (ROTA, small["rota"], "in_small"), (IDENT[:], small["ident"], "in_small"),
                                   (DFTD, small["dftd"], "in_small"), (DFTS, small["dfts"], "in_small"),
                                   (WRT[:], small["wrt"], "in_small"),
                                   (BRT[:], small["brt"].partition_broadcast(P), "in_small"),
                                   (MASK[:], small["mask"], "in_small"),
                                   (REV[:], small["rev"].partition_broadcast(P), "in_small"),
                                   (LAMV, small["lam"].partition_broadcast(P), "in_small")):
                act.dma_start(dst, src).then_inc(sem(s_in), 16)
            act.wait_ge(sem("eps"), 1)
            act.wait_ge(sem("in_x"), 16)
            norm_squares(0)
            after(-1)
            norm_result(0)
            ps = filled(act, "q")
            free(f(QL[:, 0:KL, :], ps[:, :].rearrange("p (a t) -> p a t", a=2), ACT.Copy), "q")
            after(PA["win_q"])
            ps = filled(act, "kv")
            free(f(QL[:, KL:2 * KL, :], ps[:, :].rearrange("p (a t) -> p a t", a=2), ACT.Copy), "kv")
            after(PA["win_kv"])
            ps = filled(act, "kr")
            free(f(QK[NOPE:QKD, 8, :], ps[NOPE:QKD, 0:S], ACT.Copy), "kr")
            act.wait_ge(s_fa, tiles["kv", 0][2][1])
            act.wait_ge(s_y, NCH)
            f(XR[:, 0:4, :], QL, ACT.Square).then_inc(sem("lat_sq"), 1)
            ps = filled(act, "sslat")
            free(f(RT[:, :], ps[:, :], ACT.Sqrt, bias=EPSC[:, 0:1], scale=1.0 / LORA), "sslat")
            after(PA["win_f"])
            after(PA["win_f"] + 1)
            act.wait_ge(sem("lam_dot"), 1)
            f(LAMT[:, 2:4], LAMT[:, 0:2], ACT.Exp).then_inc(sem("lam_exp"), 1)
            act.wait_ge(sem("ang"), 1)
            f(CSA, ANG, ACT.Sin).then_inc(sem("csa"), 1)
            for q in range(8):
                ps = filled(act, "g", q)
                for b in range(2):
                    j = 2 * q + b
                    last = f(G[:, j, :], ps[:, b * S:(b + 1) * S], ACT.Sigmoid,
                             bias=V[:, VCOL["b_gates"] + j:VCOL["b_gates"] + j + 1])
                free(last, "g", q)
                after(PA["win_g"] + q)
            for t in range(4):
                ps = filled(act, f"qh{t}")
                free(f(QK[:, 2 * t:2 * t + 2, :], ps[0:QKD, :].rearrange("p (a t) -> p a t", a=2), ACT.Copy,
                       scale=float(QKD) ** -0.5), f"qh{t}")
            for name in ("uq", "uk", "uv"):
                after(PA[name])

            def exp1(h):
                act.wait_ge(sem("mx1"), h + 1)
                ps = bank(f"s{h}")
                for qb in range(TB):
                    c = 4 * (h % 2) + qb
                    last = soft_exp(P1[:, h % 2, qb, :], ps[:, qb * S:(qb + 1) * S], ST[:, c:c + 1], ST[:, c + 2:c + 3])
                last.then_inc(sem("exp1"), 1)

            def copy1(h):
                ps = filled(act, f"pt{h}")
                f(PT1[:, h % 2, :, :], ps[:, :].rearrange("p (a t) -> p a t", a=2), ACT.Copy).then_inc(sem("pt1"), 1)

            for h in range(H1 + 1):
                if h < H1:
                    exp1(h)
                if h >= 1:
                    copy1(h - 1)
            for q in range(4):
                after(PA["br"] + q)

            def residual_chunk(name, page=None):
                def wait(c):
                    act.wait_ge(s_fd, tiles[name, c][2][1])
                    if page is not None and c < NCH - 1:
                        after(page + c)
                return wait

            norm(1, residual_chunk("wout", PA["wout"]))
            after(PA["wout"] + 3)
            act.wait_ge(sem("rt_gd"), 1)
            link(f(RW[:, 1, 0:8], RW[:, 1, 0:8], ACT.Exp))
            act.wait_ge(sem("rt_d2"), 1)
            f(RW[:, 1, 8:10], RW[:, 1, 8:10], ACT.Exp).then_inc(sem("rt_exp"), 1)
            act.wait_ge(sem("comb"), 1)
            act.dma_start(CT[:], acts[1]).then_inc(sem("in_ctx"), 16)

            def context_squares():
                act.wait_ge(sem("in_ctx"), 16)
                norm_squares(2)

            ff_pass("moe", (context_squares, lambda: norm_result(2)))
            norm(3, residual_chunk("acc_moe"))
            norm_squares(4)
            ff_pass("ctx_ff", (lambda: norm_result(4),))
            norm_squares(5, residual_chunk("acc_ctx"))
            ff_pass("ff00", (lambda: norm_result(5),))
            norm_squares(6, residual_chunk("acc_00"))
            for dst, src in ((BT0, small["bt"][:, 0:BTN]), (BT1, small["bt"][:, BTN:]), (CSB, small["csb"]),
                             (ROTB[:], small["rotb"])):
                act.dma_start(dst, src).then_inc(sem("in_mid"), 16)

            def two(ps):
                return ps[:, :].rearrange("p (a t) -> p a t", a=2)

            def queries(kind, base):
                for q in range(2):
                    free(f(QA[:, 2 * q:2 * q + 2, :], two(filled(act, f"q{kind}", q)), ACT.Copy, scale=HD ** -0.5),
                         f"q{kind}", q)
                    after(base + q)

            def key_half(nm, i, q, c):
                free(f(KA[:, 2 * q:2 * q + 2, c * S:(c + 1) * S], two(filled(act, nm, i)), ACT.Copy), nm, i)

            key_half("kac0", 0, 0, 1)
            norm_result(6)
            key_half("kac1", 0, 1, 1)
            for q in range(2):
                key_half("kax", q, q, 0)
                after(PA["proj_a"] + q)
            for q in range(2):
                after(PA["proj_a"] + 2 + q)
            queries("a", PA["proj_a"] + 4)
            for a in range(NA_N + 1):
                if a < NA_N:
                    act.wait_ge(sem("mx2"), a + 1)
                    c = 4 * (a % 2)
                    soft_exp(P2[:, a % 2, 0, :], bank(f"sa{a}")[:, :], ST[:, c:c + 1], ST[:, c + 2:c + 3])\
                        .then_inc(sem("exp2"), 1)
                if a >= 1:
                    b = a - 1
                    ps = filled(act, f"pta{b}")
                    h, qb = b // TB, b % TB
                    f(PT2[:, h % 2, :, qb * P:(qb + 1) * P], ps[:, :].rearrange("p (a t) -> p a t", a=NKT), ACT.Copy)\
                        .then_inc(sem("pt2"), 1)
            queries("b", PA["proj_b"])
            for q in range(2):
                for c in range(2):
                    key_half(f"kb{q}", c, q, c)
                after(PA["proj_b"] + 2 + q)
            for q in range(2):
                after(PA["proj_b"] + 4 + q)
            for a in range(DF_N + 1):
                if a < DF_N:
                    for mp in range(2):
                        act.wait_ge(sem("mx3"), 2 * a + mp + 1)
                        c = 4 * (a % 2) + mp
                        soft_exp(P2[:, a % 2, mp, :], bank(f"sd{2 * a + mp}")[:, :], ST[:, c:c + 1], ST[:, c + 2:c + 3])\
                            .then_inc(sem("exp3"), 1)
                if a >= 1:
                    b = a - 1
                    ps = filled(act, f"ptd{b}")
                    h, qb = b // TB, b % TB
                    f(PT2[:, h % 2, :, qb * P:(qb + 1) * P], ps[:, :].rearrange("p (a t) -> p a t", a=NKT), ACT.Copy)\
                        .then_inc(sem("pt3"), 1)
            for t in range(2):
                act.wait_ge(s_fd, tiles[f"od{2 * t + 1}", 0][2][1])
                if t == 0:
                    act.wait_ge(sem("na_split"), 1)
                f(XR[:, 2 * t:2 * t + 2, :], MG[:, 2 * t:2 * t + 2, :], ACT.Square).then_inc(sem("sub_sq"), 1)
            for t in range(2):
                ps = filled(act, "sssub", t)
                if t == 1:
                    act.wait_ge(sem("sub_norm"), 1)
                free(f(RT[:, :], ps[:, :], ACT.Sqrt, bias=EPSC[:, 0:1], scale=1.0 / P), "sssub", t)
            norm(7, residual_chunk("aout", PA["aout"]))
            after(PA["aout"] + 3)
            ff_pass("ff01")
            norm(8, residual_chunk("acc_01"))
            ff_pass("ff10")
            norm(9, residual_chunk("acc_10"))
            for q in range(4):
                free(f(CG[:, 2 * q:2 * q + 2, :], two(filled(act, f"cg{q}")), ACT.Copy), f"cg{q}")
                after(PA["cin"] + 2 * q)
                after(PA["cin"] + 2 * q + 1)
            for q in range(4):
                after(PA["cin"] + 8 + q)
            norm(10, residual_chunk("cout", PA["cout"]))
            after(PA["cout"] + 3)
            ff_pass("ff11")
            norm(11, residual_chunk("acc_11"))
            act.wait_ge(s_yf, NCH * 12)
            act.dma_start(small["out"], XR[:]).then_inc(sem("stored"), 16)
            act.wait_ge(sem("stored"), 16)

        @block.vector
        def _(dve):
            v = nc.vector
            chain = [0]

            def link(ins):
                chain[0] += 1
                ins.then_inc(s_dc, 1)
                dve.wait_ge(s_dc, chain[0])

            def free(ins, name, i=0):
                assert tiles[name, i][2][0] == s_fd
                ins.then_inc(s_fd, 1)

            def vec(name, k, n=1):
                return V[:, VCOL[name] + k:VCOL[name] + k + n]

            def two(ps):
                return ps[:, :].rearrange("p (a t) -> p a t", a=2)

            def mod_sum(m, vectors, i=0):
                w = mraw[:, m % 2, :].rearrange("p (k n) -> p k n", k=KD)
                dve.wait_ge(mslot[m % 2], i * 16 + 16 * (m // 2 + 1))
                for k in range(KD):
                    if k:
                        dve.wait_ge(s_mx, i * 2 * (KD - 1) + ((KD - 1) * m + k))
                    for slot_v, vi in enumerate(vectors):
                        out, c = MACC[:, m % 2, slot_v, :], CA[:, k, vi:vi + 1]
                        if k == 0:
                            last = v.tensor_scalar(out, w[:, k, :], c, None, ALU.mult)
                        else:
                            last = v.scalar_tensor_tensor(out=out, in0=w[:, k, :], scalar=c, in1=out,
                                                          op0=ALU.mult, op1=ALU.add)
                    last.then_inc(s_mx if k < KD - 1 else s_macc, 1)

            def mod_take(m, i=0, nv=1):
                dve.wait_ge(s_modp, i * 2 + (m + 1))
                cols = (lambda x: x[:, bass.ds(i * 4 + 2 * m, 2), 0:nv]) if not isinstance(i, int) else \
                    (lambda x: x[:, 2 * m:2 * m + 2, 0:nv])
                v.tensor_tensor(cols(MODT), PS[MODB][:, 0:4].rearrange("p (b v) -> p b v", v=2)[:, :, 0:nv], cols(MB),
                                ALU.add).then_inc(s_modev, 1)

            def mod_step(m, vectors=(1,), i=0):
                mod_sum(m, vectors, i)
                mod_take(m - 1, i, len(vectors))

            def norm(n):
                src, dst, gname, goff, sc, sh, vi = NORMS[n]
                if n:
                    dve.wait_ge(s_yf, NCH * n)
                if sc is None:
                    v.tensor_copy(NA_[:], vec(gname, goff, KD)).then_inc(sem("norm_gain"), 1)
                else:
                    v.scalar_tensor_tensor(out=NA_[:], in0=MODT[:, sc:sc + KD, vi], scalar=1.0,
                                           in1=vec(gname, goff, KD), op0=ALU.add, op1=ALU.mult)\
                        .then_inc(sem("norm_gain"), 1)
                dve.wait_ge(sem("norm_gain"), n + 1)
                dve.wait_ge(*tiles[f"ss{n}", 0][2])
                v.reciprocal(RT[:, 0:S], RT[:, 0:S]).then_inc(s_ri, 1)
                dve.wait_ge(s_ri, n + 1)
                for c in range(NCH + 2):
                    if c < NCH:
                        v.tensor_tensor(XR[:, 2 * c:2 * c + 2, :], src[:, 2 * c:2 * c + 2, :],
                                        RT[:, 0:S].unsqueeze(1).broadcast_to([P, 2, S]), ALU.mult).then_inc(s_xr, 1)
                    if c >= 2 and dst in OPERANDS:
                        dve.wait_ge(s_yf, NCH * n + c - 1)
                        k = slice(2 * c - 4, 2 * c - 2)
                        split(XR[:, k, :], OPERANDS[dst], k).then_inc(s_y, 1)

            def split(x, pair, k):
                link(v.tensor_copy(pair[0][:, k, :], x))
                return v.tensor_tensor(pair[1][:, k, :], x, pair[0][:, k, :].bitcast(f32), ALU.subtract)

            def residual(name, coef):
                dst, col = coef
                for q in range(4):
                    ps = filled(dve, name, q)
                    for b in range(2):
                        k = 2 * q + b
                        last = v.scalar_tensor_tensor(out=dst[:, k, :], in0=ps[:, b * S:(b + 1) * S], scalar=col(k),
                                                      in1=dst[:, k, :], op0=ALU.mult, op1=ALU.add)
                    free(last, name, q)

            def modcol(c, vi=0):
                return lambda k: MODT[:, c + k, vi:vi + 1]

            def half_gate(c, vi=0):
                link(v.tensor_scalar(HG[:], MODT[:, c:c + KD, vi], 0.5, None, ALU.mult))
                return lambda k: HG[:, k:k + 1]

            def ff_pass(name, between=()):
                p0, u0, n, src, routed, acc, parts = PASSES[name]
                steps = 3 if routed else 2
                hx0 = hx[0]

                def mask(e):
                    v.tensor_scalar(CMASK, COMBT, IDENT[0:NEXP, bass.ds(e, 1)], None, ALU.mult)\
                        .then_inc(sem("cmask"), 1)

                if routed:
                    mask(0)

                def unit(u, i, vectors):
                    U = u0 + u
                    for j in range(2):
                        done = [hx0 + steps * (2 * u + j)]

                        def step(ins):
                            done[0] += 1
                            ins.then_inc(s_hx, 1)
                            dve.wait_ge(s_hx, i * 4 * steps + done[0])

                        dve.wait_ge(s_silu, i * 4 + (2 * U + j + 1))
                        hid = SIL[:, j, :]
                        step(v.tensor_tensor(hid, PS[GU[j]][:, S:2 * S], hid, ALU.mult))
                        if routed:
                            step(v.tensor_tensor(hid, PS[MISC][:, 0:S], hid, ALU.mult))
                        step(v.tensor_copy(HH[:, j, :], hid))
                        v.tensor_tensor(HL[:, j, :], hid, HH[:, j, :].bitcast(f32), ALU.subtract).then_inc(s_hid, 1)
                        if routed and j == 1:
                            mask(i * 2 + (u + 1))
                    if vectors:
                        mod_step(MOD_AT[name] + u, vectors, i)

                units(dve, parts, unit, between)
                hx[0] += steps * 2 * n

            hx = [0]

            v.memset(EPSC[:], EPS).then_inc(sem("eps"), 1)
            v.memset(ZW[:], 0.0)
            v.memset(SIL[:, 0, :], 0.0).then_inc(s_hid, 1)
            v.memset(SIL[:, 1, :], 0.0).then_inc(s_hid, 1)
            v.memset(MACC[:], 0.0)
            v.memset(ONES[:], 1.0).then_inc(sem("ones"), 1)
            dve.wait_ge(sem("ones"), 1)
            dve.wait_ge(sem("in_mb"), 16)
            dve.wait_ge(sem("in_vecs"), 16)

            dve.wait_ge(sem("silu_c"), 1)
            mod_sum(0, (0,))
            for m in range(1, MOD_AT["gates"]):
                mod_step(m, (0,))
            mod_take(MOD_AT["gates"] - 1)
            dve.wait_ge(s_modev, MOD_AT["gates"])
            norm(0)
            dve.wait_ge(sem("in_small"), 16 * N_SMALL)
            for t in range(2):
                link(v.tensor_tensor(LAMV[:, 2 * t, :], LAMV[:, 2 * t, :], LAMV[:, 2 * t + 1, :], ALU.mult))
            v.tensor_reduce(LAMT[:, 0:2], LAMV[:, 0:4:2, :], AX.X, ALU.add).then_inc(sem("lam_dot"), 1)
            link(v.tensor_copy(AK[:, 0, :], POSI))
            link(v.tensor_scalar(ANG[:, 0, :], AK[:, 0, :], INVF[:, 0:1], None, ALU.mult))
            link(v.tensor_copy(ANG[:, 1, :], ANG[:, 0, :]))
            MAGIC = 1.5 * 2.0 ** 23
            link(v.tensor_scalar(AK[:, 0, :], ANG[:, 0, :], 1.0 / (2.0 * np.pi), 0.25, ALU.mult, ALU.add))
            link(v.tensor_scalar(AK[:, 1, :], ANG[:, 1, :], 1.0 / (2.0 * np.pi), None, ALU.mult))
            link(v.tensor_scalar(AK, AK, MAGIC, None, ALU.add))
            link(v.tensor_scalar(AK, AK, MAGIC, None, ALU.subtract))
            two_pi = 2.0 * np.pi
            parts = []
            rest = two_pi
            for scale in (2.0 ** 5, 2.0 ** 13, 2.0 ** 21):
                part = np.round(rest * scale) / scale
                parts.append(float(part))
                rest -= part
            parts.append(float(np.float32(rest)))
            for part in parts:
                link(v.scalar_tensor_tensor(out=ANG, in0=AK, scalar=-part, in1=ANG, op0=ALU.mult, op1=ALU.add))
            link(v.tensor_scalar(ANG[:, 0, :], ANG[:, 0, :], float(np.pi / 2), None, ALU.add))
            PI = float(np.nextafter(np.float32(np.pi), np.float32(0)))
            v.tensor_scalar(ANG, ANG, PI, -PI, ALU.min, ALU.max).then_inc(sem("ang"), 1)

            for q in range(2):
                free(v.tensor_copy(FT[:, 2 * q:2 * q + 2, :], two(filled(dve, "f", q))), "f", q)
            v.memset(QK[0:NOPE, 8, :], 0.0).then_inc(sem("kr_zero"), 1)
            dve.wait_ge(*tiles["sslat", 0][2])
            link(v.reciprocal(RT[:], RT[:]))
            for half in range(2):
                for t in range(2 * half, 2 * half + 2):
                    g = vec("g_q", t) if t < KL else vec("g_kv", t - KL)
                    last = v.scalar_tensor_tensor(out=QL[:, t, :], in0=QL[:, t, :], scalar=g,
                                                  in1=RT[:, half * S:(half + 1) * S], op0=ALU.mult, op1=ALU.mult)
                link(last)
                k = slice(2 * half, 2 * half + 2)
                split(QL[:, k, :], OPERANDS["yc"], k).then_inc(sem("lat_n"), 1)
            m = MOD_AT["gates"]
            mod_sum(m, (0,))
            for m in range(m + 1, m + 10):
                mod_step(m, (0,))
            for t in range(2):
                ps = filled(dve, f"kh{t}")
                for odd in range(2):
                    last = v.tensor_copy(KH[0:NOPE, 4 * t + odd:4 * t + 4:2, :],
                                         ps[odd * NOPE:(odd + 1) * NOPE, :].rearrange("p (a t) -> p a t", a=2))
                free(last, f"kh{t}")
            mod_step(m + 1, (0,))
            for t in range(TB):
                free(v.tensor_copy(V1[:, t, :], filled(dve, f"v{t}")[:, :]), f"v{t}")
            mod_step(m + 2, (0,))
            link(v.tensor_scalar(LAMT[:, 5:6], vec("subln", 0), 1.0 - LAM_INIT, None, ALU.mult))
            dve.wait_ge(sem("lam_exp"), 1)
            link(v.tensor_tensor(LAMT[:, 4:5], LAMT[:, 2:3], LAMT[:, 3:4], ALU.subtract))
            link(v.tensor_scalar(LAMT[:, 4:5], LAMT[:, 4:5], LAM_INIT, None, ALU.add))
            filled(dve, "rot", 4)
            dve.wait_ge(sem("csa"), 1)
            link(v.tensor_tensor(QK, QK, CSA[:, 0:1, :].broadcast_to([QKD, 9, S]), ALU.mult))
            for t in range(5):
                w = 2 if t < 4 else 1
                ps = bank("rot", t)[0:QKD, 0:w * S].rearrange("p (a t) -> p a t", a=w)
                tmp = XR[0:QKD, 0:w, :]
                link(v.tensor_tensor(tmp, ps, CSA[:, 1:2, :].broadcast_to([QKD, w, S]), ALU.mult))
                free(v.tensor_tensor(QK[:, 2 * t:2 * t + w, :], QK[:, 2 * t:2 * t + w, :], tmp, ALU.add), "rot", t)
                dve.wait_ge(*tiles["rot", t][2])
            mod_step(MOD_AT["moe"] - 1, (0,))
            v.tensor_copy(KH[NOPE:QKD, :, :], QK[NOPE:QKD, 8:9, :].broadcast_to([ROPE, H1, S])).then_inc(sem("rope1"), 1)

            def max1(h):
                ps = filled(dve, f"s{h}")
                c = 4 * (h % 2)
                v.tensor_reduce(ST[:, c:c + 2], two(ps), AX.X, ALU.max, negate=True).then_inc(sem("mx1"), 1)

            def norm1(h):
                c = 4 * (h % 2)
                dve.wait_ge(sem("exp1"), h + 1)
                link(v.reciprocal(ST[:, c + 2:c + 4], ST[:, c + 2:c + 4]))
                v.tensor_tensor(P1[:, h % 2, :, :], P1[:, h % 2, :, :],
                                ST[:, c + 2:c + 4].unsqueeze(2).broadcast_to([P, TB, S]), ALU.mult)\
                    .then_inc(sem("pn1"), 1)

            for h in range(H1 + 2):
                if h < H1:
                    max1(h)
                if 1 <= h <= H1:
                    norm1(h - 1)
                if h >= 2:
                    if (h - 2) % 2 == 1:
                        pr = (h - 2) // 2
                        free(split(filled(dve, f"o{pr}")[:, 0:S], OPERANDS["y"], pr), f"o{pr}")
            dve.wait_ge(s_fd, tiles["o3", 0][2][1])
            v.memset(ST[:, 31:32], 0.0).then_inc(sem("at_done"), 4)
            for t in range(4):
                tb, fp = t // 2, t % 2
                ps = filled(dve, "fd", t)
                free(v.tensor_copy(U2[:, tb, :, fp * S:(fp + 1) * S].rearrange("p c (q n) -> p q c n", q=2),
                                   ps[:, :].rearrange("p (q c n) -> p q c n", q=2, c=2)), "fd", t)
            for t in range(2):
                free(split(two(filled(dve, "fs", t)), OPERANDS["y"], slice(4 + 2 * t, 6 + 2 * t)), "fs", t)
            dve.wait_ge(*tiles["fs", 1][2])
            v.memset(ST[:, 30:31], 0.0).then_inc(sem("fo_done"), 2)
            dve.wait_ge(s_fa, tiles["g", 7][2][1])
            for q in range(4):
                ps = filled(dve, "bra", q)
                free(v.tensor_tensor(G[:, 2 * q:2 * q + 2, :], two(ps), G[:, 2 * q:2 * q + 2, :], ALU.mult), "bra", q)
            for q in range(4):
                ps = filled(dve, "brf", q)
                free(v.tensor_tensor(G[:, 8 + 2 * q:10 + 2 * q, :], two(ps), G[:, 8 + 2 * q:10 + 2 * q, :], ALU.mult), "brf", q)
            for q in range(4):
                dve.wait_ge(*tiles["brf", q][2])
                k = slice(2 * q, 2 * q + 2)
                link(v.tensor_tensor(G[:, k, :], G[:, k, :], G[:, 8 + 2 * q:10 + 2 * q, :], ALU.add))
                split(G[:, k, :], OPERANDS["yc"], k).then_inc(sem("merged"), 1)
            dve.wait_ge(s_modev, MOD_AT["moe"] - 1)
            residual("wout", (HT, modcol(ADA + 16)))
            norm(1)

            LG = RW[:, 0, 0:2 * 36].rearrange("p (t n) -> p t n", t=TB)

            def rw(i, *dims, off=0):
                n = int(np.prod(dims))
                a = RW[:, i, off:off + n]
                if len(dims) == 2:
                    return a.rearrange("p (a b) -> p a b", a=dims[0])
                if len(dims) == 3:
                    return a.rearrange("p (a b c) -> p a b c", a=dims[0], b=dims[1])
                return a

            def over(x, n):
                return x.unsqueeze(2).broadcast_to([P, TB, n])

            ps = filled(dve, "rt")
            free(v.tensor_tensor(LG, ps[:, 0:TB * 64].rearrange("p (t n) -> p t n", t=TB)[:, :, 0:36],
                                 BRT[:].unsqueeze(1).broadcast_to([P, TB, 36]), ALU.add), "rt")
            dve.wait_ge(*tiles["rt", 0][2])
            ge = rw(1, TB, NG)
            gm, gs = RW[:, 6, 0:2], RW[:, 6, 2:4]
            eq = rw(2, TB, NG)
            oh = rw(3, TB, NG)
            rev4 = REV[:, 4:8].unsqueeze(1).broadcast_to([P, TB, NG])
            rev8 = REV[:].unsqueeze(1).broadcast_to([P, TB, NE8])
            link(v.tensor_reduce(gm, LG[:, :, 0:NG], AX.X, ALU.max))
            link(v.tensor_tensor(ge, LG[:, :, 0:NG], over(gm, NG), ALU.subtract))
            link(v.scalar_tensor_tensor(out=eq, in0=ge, scalar=0.0, in1=rev4, op0=ALU.is_ge, op1=ALU.mult))
            link(v.tensor_reduce(gs, eq, AX.X, ALU.max))
            v.tensor_tensor(oh, eq, over(gs, NG), ALU.is_equal).then_inc(sem("rt_gd"), 1)
            dve.wait_ge(sem("rt_gd"), 1)
            big = rw(4, TB, NG, NE8)
            link(v.tensor_tensor(big, LG[:, :, NG:].rearrange("p t (g e) -> p t g e", g=NG),
                                 oh.unsqueeze(3).broadcast_to([P, TB, NG, NE8]), ALU.mult))
            el = rw(5, TB, NE8)
            link(v.tensor_reduce(el, big.rearrange("p t g e -> p t e g"), AX.X, ALU.add))
            m1, pm = RW[:, 6, 4:6], RW[:, 6, 6:8]
            d1, oh1, oh2 = rw(2, TB, NE8, off=16), rw(3, TB, NE8, off=16), rw(3, TB, NE8, off=32)
            link(v.tensor_reduce(m1, el, AX.X, ALU.max))
            link(v.tensor_tensor(d1, el, over(m1, NE8), ALU.is_equal))
            link(v.tensor_tensor(d1, d1, rev8, ALU.mult))
            link(v.tensor_reduce(pm, d1, AX.X, ALU.max))
            link(v.tensor_tensor(oh1, d1, over(pm, NE8), ALU.is_equal))
            link(v.scalar_tensor_tensor(out=el, in0=oh1, scalar=NEG, in1=el, op0=ALU.mult, op1=ALU.add))
            m2 = RW[:, 6, 8:10]
            link(v.tensor_reduce(m2, el, AX.X, ALU.max))
            link(v.tensor_tensor(d1, el, over(m2, NE8), ALU.is_equal))
            link(v.tensor_tensor(d1, d1, rev8, ALU.mult))
            link(v.tensor_reduce(pm, d1, AX.X, ALU.max))
            link(v.tensor_tensor(oh2, d1, over(pm, NE8), ALU.is_equal))
            v.tensor_tensor(RW[:, 1, 8:10], m2, m1, ALU.subtract).then_inc(sem("rt_d2"), 1)
            dve.wait_ge(sem("rt_exp"), 1)
            w1, w2, gp = RW[:, 6, 10:12], RW[:, 6, 12:14], RW[:, 6, 14:16]
            link(v.tensor_reduce(gp, ge, AX.X, ALU.add))
            link(v.reciprocal(gp, gp))
            link(v.tensor_scalar(w1, RW[:, 1, 8:10], 1.0, None, ALU.add))
            link(v.reciprocal(w1, w1))
            link(v.tensor_tensor(w2, w1, RW[:, 1, 8:10], ALU.mult))
            link(v.tensor_tensor(w1, w1, gp, ALU.mult))
            link(v.tensor_tensor(w2, w2, gp, ALU.mult))
            link(v.tensor_tensor(oh1, oh1, over(w1, NE8), ALU.mult))
            link(v.tensor_tensor(oh2, oh2, over(w2, NE8), ALU.mult))
            link(v.tensor_tensor(oh1, oh1, oh2, ALU.add))
            for t in range(TB):
                cw = RW[:, 7, t * NEXP:(t + 1) * NEXP].rearrange("p (g e) -> p g e", g=NG)
                last = v.tensor_tensor(cw, oh[:, t, :].unsqueeze(2).broadcast_to([P, NG, NE8]),
                                       oh1[:, t:t + 1, :].broadcast_to([P, NG, NE8]), ALU.mult)
                if t == 0:
                    link(last)
            last.then_inc(sem("comb"), 1)
            free(v.tensor_copy(COMBT, filled(dve, "ct")[0:NEXP, 0:S]), "ct")
            dve.wait_ge(*tiles["ct", 0][2])
            ff_pass("moe", (lambda: None, lambda: norm(2)))
            residual("acc_moe", (HT, modcol(ADA + 40)))
            norm(3)

            ff_pass("ctx_ff", (lambda: norm(4),))
            residual("acc_ctx", (CT, half_gate(MOD0 + 16, 1)))
            ff_pass("ff00", (lambda: norm(5),))
            residual("acc_00", (HT, half_gate(MOD0 + 16, 0)))
            mod_take(MOD_AT["mixer"] - 1)
            norm(6)
            for q in range(2):
                for c in range(2):
                    ps = filled(dve, f"va{q}", c)
                    free(v.tensor_copy(VA[:, 2 * c:2 * c + 2, q * S:(q + 1) * S], two(ps)), f"va{q}", c)
            dve.wait_ge(sem("in_mid"), 16 * N_MID)
            for h in range(NA_H):
                last = v.tensor_tensor(bias_of(h), bias_of(h), MASK[:].unsqueeze(1).broadcast_to([P, 6, GRID]), ALU.add)
            link(last)

            def maxa(a):
                h, qb = a // TB, a % TB
                ps = filled(dve, f"sa{a}")
                c = 4 * (a % 2)
                link(v.tensor_tensor(ps[:, 0:S].rearrange("p (r c) -> p r c", c=GRID),
                                     ps[:, 0:S].rearrange("p (r c) -> p r c", c=GRID),
                                     bias_of(h)[:, 2 - 2 * qb:6 - 2 * qb, :], ALU.add))
                v.tensor_reduce(ST[:, c:c + 1], ps[:, :], AX.X, ALU.max, negate=True).then_inc(sem("mx2"), 1)

            def norma(a):
                c = 4 * (a % 2)
                dve.wait_ge(sem("exp2"), a + 1)
                link(v.reciprocal(ST[:, c + 2:c + 3], ST[:, c + 2:c + 3]))
                v.tensor_scalar(P2[:, a % 2, 0, :], P2[:, a % 2, 0, :], ST[:, c + 2:c + 3], None, ALU.mult)\
                    .then_inc(sem("pn2"), 1)

            for a in range(NA_N + 2):
                if a < NA_N:
                    maxa(a)
                if 1 <= a <= NA_N:
                    norma(a - 1)
                if a >= 2 and (a - 2) % 4 == 3:
                    pr = (a - 2) // 4
                    free(v.tensor_copy(XR[:, pr, :], filled(dve, f"oa{pr}")[:, 0:S]), f"oa{pr}")
            for q in range(2):
                for c in range(2):
                    ps = filled(dve, f"vb{q}", c)
                    free(v.tensor_copy(VA[:, 2 * c:2 * c + 2, q * S:(q + 1) * S], two(ps)), f"vb{q}", c)
            for t in range(4):
                ps = filled(dve, "rotb", t)
                x = QA[:, 2 * t:2 * t + 2, :] if t < 2 else KA[:, 2 * (t - 2):2 * (t - 2) + 2, 0:S]
                tmp = P2[:, 0, 0, :].rearrange("p (a t) -> p a t", a=2)
                link(v.tensor_tensor(x, x, CSB[:, 0:1, :].broadcast_to([P, 2, S]), ALU.mult))
                link(v.tensor_tensor(tmp, two(ps), CSB[:, 1:2, :].broadcast_to([P, 2, S]), ALU.mult))
                free(v.tensor_tensor(x, x, tmp, ALU.add), "rotb", t)
                dve.wait_ge(*tiles["rotb", t][2])
            v.memset(ST[:, 31:32], 0.0).then_inc(sem("rope2"), 1)
            split(XR[:, 0:4, :], OPERANDS["y"], slice(0, 4)).then_inc(sem("na_split"), 1)
            def maxd(a):
                for mp in range(2):
                    ps = filled(dve, f"sd{2 * a + mp}")
                    c = 4 * (a % 2) + mp
                    v.tensor_reduce(ST[:, c:c + 1], ps[:, :], AX.X, ALU.max, negate=True).then_inc(sem("mx3"), 1)

            def normd(a):
                c = 4 * (a % 2)
                dve.wait_ge(sem("exp3"), 2 * a + 2)
                link(v.reciprocal(ST[:, c + 2:c + 4], ST[:, c + 2:c + 4]))
                link(v.tensor_tensor(ST[:, c + 3:c + 4], ST[:, c + 3:c + 4], LAMT[:, 4:5], ALU.mult))
                link(v.tensor_scalar(P2[:, a % 2, 1, :], P2[:, a % 2, 1, :], ST[:, c + 3:c + 4], None, ALU.mult))
                v.scalar_tensor_tensor(out=P2[:, a % 2, 0, :], in0=P2[:, a % 2, 0, :], scalar=ST[:, c + 2:c + 3],
                                       in1=P2[:, a % 2, 1, :], op0=ALU.mult, op1=ALU.subtract)\
                    .then_inc(sem("pn3"), 1)

            for a in range(DF_N + 2):
                if a < DF_N:
                    maxd(a)
                if 1 <= a <= DF_N:
                    normd(a - 1)
                if a >= 2 and (a - 2) % 2 == 1:
                    h = (a - 2) // 2
                    free(v.tensor_copy(MG[:, h, :], filled(dve, f"od{h}")[:, 0:S]), f"od{h}")
            mod_sum(MOD_AT["mixer"], (1,))
            for t in range(2):
                dve.wait_ge(*tiles["sssub", t][2])
                k = slice(2 * t, 2 * t + 2)
                link(v.reciprocal(RT[:], RT[:]))
                link(v.scalar_tensor_tensor(out=MG[:, k, :], in0=MG[:, k, :], scalar=LAMT[:, 5:6], in1=two(RT),
                                            op0=ALU.mult, op1=ALU.mult))
                split(MG[:, k, :], OPERANDS["y"], slice(4 + 2 * t, 6 + 2 * t)).then_inc(sem("sub_norm"), 1)
            residual("aout", (HT, modcol(MOD0 + 40)))
            norm(7)
            ff_pass("ff01")
            residual("acc_01", (HT, half_gate(MOD0 + 64, 0)))
            norm(8)
            ff_pass("ff10")
            residual("acc_10", (HT, half_gate(MOD1 + 16, 0)))
            norm(9)
            link(v.memset(UU[:, :, 0:1], 0.0))
            link(v.memset(UU[:, :, S + 1:S + 2], 0.0))
            for q in range(4):
                ps = filled(dve, f"ch{q}")
                dve.wait_ge(*tiles[f"cg{q}", 0][2])
                free(v.tensor_tensor(UU[:, 2 * q:2 * q + 2, 1:S + 1], two(ps), CG[:, 2 * q:2 * q + 2, :], ALU.mult), f"ch{q}")
                mod_step(MOD_AT["cin"] + q)
            dve.wait_ge(*tiles["ch3", 0][2])
            for tap in range(3):
                for k in range(KD):
                    w = vec("conv_w", 8 * tap + k)
                    if tap == 0:
                        last = v.tensor_scalar(VV[:, k, :], UU[:, k, 0:S], w, None, ALU.mult)
                    else:
                        last = v.scalar_tensor_tensor(out=VV[:, k, :], in0=UU[:, k, tap:tap + S], scalar=w,
                                                      in1=VV[:, k, :], op0=ALU.mult, op1=ALU.add)
                link(last)
            for q in range(4):
                ps = filled(dve, "cb", q)
                k = slice(2 * q, 2 * q + 2)
                free(v.tensor_tensor(BV[:, k, :], two(ps), VV[:, k, :], ALU.mult), "cb", q)
                dve.wait_ge(*tiles["cb", q][2])
                split(BV[:, k, :], OPERANDS["yc"], k).then_inc(sem("bv_done"), 1)
                if q < 2:
                    mod_step(MOD_AT["cin"] + 4 + q)
                elif q == 2:
                    mod_take(NMODP - 1)
            residual("cout", (HT, modcol(MOD1 + 40)))
            norm(10)
            ff_pass("ff11")
            residual("acc_11", (HT, half_gate(MOD1 + 64, 0)))
            norm(11)


def _page_k(w):
    k, n = w.shape
    return w.reshape(k // P, P, n // FU, FU).transpose(2, 1, 0, 3).reshape(n // FU, P, PAGE)


def _ff_pages(g, u, d):
    n = g.shape[1] // FU
    gu = np.stack([g.reshape(KD, P, n, 2, P), u.reshape(KD, P, n, 2, P)], axis=4)
    gu = gu.transpose(2, 3, 1, 0, 4, 5).reshape(n, 2, P, PAGE)
    dn = d.reshape(n, 2, P, D).transpose(0, 2, 1, 3).reshape(n, 1, P, PAGE)
    return np.concatenate([gu, dn], axis=1)


def _cols(x):
    return np.ascontiguousarray(x, dtype=np.float32).reshape(-1, P).T


def kernel(**inputs):
    import concourse.bacc as _bacc
    from concourse.bass_utils import run_bass_kernel_spmd as _run

    a = {k: np.asarray(v) for k, v in inputs.items()}
    pg = np.zeros((NPAGES, P, PAGE), np.float32)

    def put(name, x, at=0, width=PAGE):
        p = PAGE_AT[name] + at
        pg[p:p + len(x), :, 0:width] = x

    ada, fin, mod = _page_k(a["w_ada"][0]), _page_k(a["w_ada_final"]), [_page_k(a["mod_w_2"][i]) for i in range(2)]
    w_in = a["w_in"][0]
    mpg = np.concatenate([ada, fin, mod[0], mod[1]])
    put("win_q", _page_k(w_in[:, 0:256]))
    put("win_kv", _page_k(w_in[:, 256:512]))
    put("win_f", _page_k(w_in[:, 544:1056]))
    put("win_g", _page_k(w_in[:, 1056:]))
    for name, key in (("uq", "w_uq"), ("uk", "w_uk"), ("uv", "w_uv")):
        w = a[key][0].reshape(KL, P, -1).transpose(1, 0, 2).reshape(1, P, -1)
        put(name, w, width=w.shape[2])
    for i, key in enumerate(("w_branch_attn", "w_branch_fourier")):
        w = a[key][0].reshape(4, P, 2, 512).transpose(2, 1, 0, 3).reshape(2, P, PAGE)
        put("br", w, at=2 * i)
    put("wout", _page_k(a["w_out"][0]))

    def ff(name, units):
        put(name, units.reshape(-1, P, PAGE))

    moe = np.concatenate([_ff_pages(a["w_expert_gate"][0, e], a["w_expert_up"][0, e], a["w_expert_down"][0, e])
                          for e in range(NEXP)])
    ffw = [[_ff_pages(a["ffn_w_gate_2"][i, j], a["ffn_w_up_2"][i, j], a["ffn_w_down_2"][i, j])
            for j in range(2)] for i in range(2)]
    ff("moe", moe)
    ff("ctx_ff", ffw[0][0])
    ff("ff00", ffw[0][0])
    ff("ff01", ffw[0][1])
    ff("ff10", ffw[1][0])
    ff("ff11", ffw[1][1])
    proj = _page_k(a["attn_w_in_2"][0])
    put("proj_a", np.concatenate([proj[2:6], proj[0:2]]))
    put("proj_b", proj[6:12])
    put("aout", _page_k(a["attn_w_out_2"][0]))
    bg, cg, hh = (_page_k(a["conv_w_in_2"][0][:, i * D:(i + 1) * D]) for i in range(3))
    put("cin", np.concatenate([np.stack([cg, hh], 1).reshape(8, P, PAGE), bg]))
    put("cout", _page_k(a["conv_w_out_2"][0]))

    def tokens(x):
        return x.reshape(S, KD, P).transpose(2, 1, 0)

    acts = np.stack([tokens(a["x"]), tokens(a["ctx_2"])])
    vecs = np.concatenate([_cols(a[k]) for k in ("g_norm_mix", "g_norm_ffn", "g_norm_final", "norm_g_2", "final_g_2",
                                                 "b_gates", "conv_w_2", "g_q_lat", "g_kv_lat", "c", "c_2", "c_ctx_2",
                                                 "diff_subln_g_2")], axis=1)
    mb = np.concatenate([_cols(a["b_ada"]), _cols(a["b_ada_final"]), _cols(a["mod_b_2"])], axis=1)
    mb = np.stack([mb, mb], axis=2)

    f32 = np.float32
    rota = np.zeros((QKD, QKD), f32)
    for i in range(ROPE // 2):
        rota[NOPE + ROPE // 2 + i, NOPE + i] = -1.0
        rota[NOPE + i, NOPE + ROPE // 2 + i] = 1.0
    rotb = np.zeros((P, P), f32)
    for i in range(0, P, 2):
        rotb[i + 1, i] = -1.0
        rotb[i, i + 1] = 1.0
    invf = np.zeros((QKD, 1), f32)
    inv = np.power(f32(10000.0), -np.arange(0, ROPE, 2, dtype=f32) / f32(ROPE)).astype(f32)
    invf[NOPE:, 0] = np.concatenate([inv, inv])
    t = np.arange(S)
    inv2 = np.power(f32(10000.0), -np.arange(16, dtype=f32) / f32(16)).astype(f32)
    ang = np.concatenate([(t // GRID).astype(f32)[:, None] * inv2, (t % GRID).astype(f32)[:, None] * inv2], axis=1)
    ang = np.tile(np.repeat(ang, 2, axis=1), (1, 2)).T.astype(np.float64)
    csb = np.stack([np.cos(ang), np.sin(ang)], axis=1).astype(f32)
    th = 2 * np.pi * np.outer(np.arange(64), np.arange(64)) / 64
    dftd = np.zeros((P, 2, P), f32)
    for g in range(2):
        dftd[64 * g:64 * g + 64, 0, 64 * g:64 * g + 64] = np.cos(th)
        dftd[64 * g:64 * g + 64, 1, 64 * g:64 * g + 64] = np.sin(th)
    th = 2 * np.pi * (np.outer(t, t) % S) / S
    norm = 1.0 / np.sqrt(S * 64.0)
    dfts = (np.stack([np.cos(th), -np.sin(th)], axis=1) * norm).astype(f32)
    dfts = dfts.reshape(TB, P, 2, S).transpose(1, 0, 2, 3)
    rpb = a["na_rpb_2"][0]
    pad = np.zeros((NA_H, 15, 48 + 31 + 48), f32)
    pad[:, :, 48:79] = rpb
    bt = np.zeros((P, NA_H, 6, GRID), f32)
    for qc in range(GRID):
        strip = pad[:, :, 63 - qc:127 - qc]
        bt[qc] = strip[:, 5:11]
        bt[GRID + qc] = strip[:, 4:10]
    qc = np.arange(GRID)
    cs = np.clip(qc - 8, 0, GRID - 16)
    ok = (qc[None, :] >= cs[:, None]) & (qc[None, :] < cs[:, None] + 16)
    mask = np.tile(np.where(ok, f32(0), f32(NEG)), (2, 1)).astype(f32)
    wkr = w_in[:, 512:544].reshape(KD, P, ROPE).transpose(1, 0, 2)
    wrt = np.concatenate([a["w_router_group"][0], a["w_router_expert"][0].reshape(D, NEXP)], axis=1)
    wrt = wrt.reshape(KD, P, NG + NEXP).transpose(1, 0, 2)
    brt = np.concatenate([a["b_router_group"].reshape(-1), a["b_router_expert"].reshape(-1)])

    smalls = {"wkr": wkr, "rota": rota, "invf": invf, "pos": a["positions"].reshape(-1), "dftd": dftd, "dfts": dfts,
              "ident": np.eye(P, dtype=f32), "wrt": wrt, "brt": brt, "rev": np.arange(8, 0, -1).astype(f32),
              "rotb": rotb, "csb": csb, "bt": bt, "mask": mask, "lam": a["diff_lambda_2"][0].reshape(4, HD)}
    arrays = {"pages": pg, "mpages": mpg, "acts": acts, "vecs": vecs, "mbias": mb, **smalls}
    arrays = {k: np.ascontiguousarray(v) for k, v in arrays.items()}
    nc = _bacc.Bacc("TRN2", target_bir_lowering=False, num_devices=1)
    ap = {k: nc.dram_tensor(f"in_{k}", v.shape, mybir.dt.from_np(v.dtype), kind="ExternalInput").ap()
          for k, v in arrays.items()}
    out = nc.dram_tensor("out_0", (P, KD, S), mybir.dt.float32, kind="ExternalOutput").ap()
    build(nc, ap["pages"], ap["mpages"], ap["acts"], ap["vecs"], ap["mbias"], {**{k: ap[k] for k in smalls}, "out": out})
    r = _run(nc, [{f"in_{k}": v for k, v in arrays.items()}], core_ids=[0])
    y = r.results[0]["out_0"]
    return y.transpose(2, 1, 0).reshape(1, S, D)
```
